# Optimizing a Trainium2 kernel written in Bass

```python
import math
import jax
import jax.numpy as jnp
from jax import lax
import numpy as np

D_MODEL = 1024
BATCH = 1
SEQ = 512
DEPTH = 2
DEC_BATCH = 8
DEC_SEQ = 16
PAST_LEN = 1024

CHUNK = 64
HEAD_DIM = 64
H_RET = 6
H_SWA = 6
KV_SWA = 2
G_SWA = H_SWA // KV_SWA
H_CA = 4
MIX_WIDTH = (H_RET + H_SWA + H_CA) * HEAD_DIM
SWA_WINDOW = 128
SWA_PREV_CHUNKS = SWA_WINDOW // CHUNK
SWA_ROWS = SWA_PREV_CHUNKS * CHUNK
CA_PREV_CHUNKS = 8
CA_ROWS = CA_PREV_CHUNKS * CHUNK
REL_CLIP = 128
N_REL = 2 * REL_CLIP + 1
D_FF = 2816
CONV_W = 3
EPS = 1e-6
ROPE_BASE = 10000.0
NEG_INF = -1e30
SPLIT_HEADS = (H_RET, H_RET, H_RET, H_RET, H_SWA, KV_SWA, KV_SWA, H_CA, H_CA, H_CA)
SPLIT_SIZES = tuple(h * HEAD_DIM for h in SPLIT_HEADS)
IN_COLS = sum(SPLIT_SIZES)

kernel_name = "hybrid_streaming_encoder_step"

def rms_norm(x, g):
    xf = x.astype(jnp.float32)
    y = xf * lax.rsqrt(jnp.mean(xf * xf, axis=-1, keepdims=True) + EPS)
    return (y * g.astype(jnp.float32)).astype(x.dtype)

def split_proj(p):
    b, l = p.shape[0], p.shape[1]
    outs = []
    start = 0
    for size, heads in zip(SPLIT_SIZES, SPLIT_HEADS):
        outs.append(p[:, :, start:start + size].reshape(b, l, heads, HEAD_DIM))
        start += size
    return outs

def rotary(x, pos):
    half = HEAD_DIM // 2
    inv = 1.0 / (ROPE_BASE ** (jnp.arange(half, dtype=jnp.float32) / half))
    ang = pos.astype(jnp.float32)[:, None] * inv[None, :]
    cos = jnp.cos(ang)[None, :, None, :]
    sin = jnp.sin(ang)[None, :, None, :]
    xf = x.astype(jnp.float32)
    x1, x2 = xf[..., :half], xf[..., half:]
    return jnp.concatenate([x1 * cos - x2 * sin, x2 * cos + x1 * sin], axis=-1).astype(x.dtype)

def ret_log_decay():
    return jnp.log(1.0 - 2.0 ** (-5.0 - jnp.arange(H_RET, dtype=jnp.float32)))

def retention_block(q, k, v, s0):
    t_len = q.shape[1]
    log_g = ret_log_decay()
    t = jnp.arange(t_len, dtype=jnp.float32)
    diff = t[:, None] - t[None, :]
    decay = jnp.where(diff >= 0, jnp.exp(jnp.maximum(diff, 0.0)[None] * log_g[:, None, None]), 0.0)
    scores = jnp.einsum('bihd,bjhd->bhij', q, k) * decay[None]
    inner = jnp.einsum('bhij,bjhd->bihd', scores, v)
    q_decay = jnp.exp((t + 1.0)[:, None] * log_g[None, :])
    cross = jnp.einsum('bihd,bhde->bihe', q, s0) * q_decay[None, :, :, None]
    k_decay = jnp.exp((t_len - 1.0 - t)[:, None] * log_g[None, :])
    s_new = (jnp.exp(t_len * log_g)[None, :, None, None] * s0
             + jnp.einsum('bjhd,bjhe->bhde', k * k_decay[None, :, :, None], v))
    return inner + cross, s_new

def retention_prompt(q, k, v):
    b, l, h, d = q.shape
    nc = l // CHUNK

    def to_chunks(x):
        return jnp.moveaxis(x.astype(jnp.float32).reshape(b, nc, CHUNK, h, d), 1, 0)

    def step(s, qkv):
        o, s_new = retention_block(qkv[0], qkv[1], qkv[2], s)
        return s_new, o

    s0 = jnp.zeros((b, h, d, d), jnp.float32)
    s_fin, o = lax.scan(step, s0, (to_chunks(q), to_chunks(k), to_chunks(v)))
    return jnp.moveaxis(o, 0, 1).reshape(b, l, h, d), s_fin

def retention_out(o, g):
    mu = jnp.mean(o, axis=-1, keepdims=True)
    var = jnp.mean(jnp.square(o - mu), axis=-1, keepdims=True)
    on = (o - mu) * lax.rsqrt(var + EPS)
    return (on * jax.nn.silu(g.astype(jnp.float32))).astype(g.dtype)

def band(x, n_prev):
    b, l = x.shape[0], x.shape[1]
    nc = l // CHUNK
    xc = x.reshape((b, nc, CHUNK) + x.shape[2:])
    xp = jnp.concatenate([jnp.zeros((b, n_prev, CHUNK) + x.shape[2:], x.dtype), xc], axis=1)
    return jnp.concatenate([xp[:, j:j + nc] for j in range(n_prev + 1)], axis=2)

def band_valid(nc, n_prev):
    cidx = jnp.arange(nc)[:, None] - n_prev + (jnp.arange((n_prev + 1) * CHUNK) // CHUNK)[None, :]
    return cidx >= 0

def sink_attention(q, k, v, valid, sinks):
    s = jnp.einsum('bnqkgd,bntkd->bnkgqt', q, k).astype(jnp.float32) * (HEAD_DIM ** -0.5)
    s = jnp.where(valid[None, :, None, None, None, :], s, NEG_INF)
    sk = sinks.astype(jnp.float32)[None, None, :, :, None, None]
    m = jnp.maximum(jnp.max(s, axis=-1, keepdims=True), sk)
    p = jnp.exp(s - m)
    denom = jnp.sum(p, axis=-1, keepdims=True) + jnp.exp(sk - m)
    return jnp.einsum('bnkgqt,bntkd->bnqkgd', (p / denom).astype(v.dtype), v)

def rel_bias_matrix(table, tq, n_before, tk):
    dist = n_before + jnp.arange(tq)[:, None] - jnp.arange(tk)[None, :]
    idx = jnp.clip(dist, -REL_CLIP, REL_CLIP) + REL_CLIP
    return jnp.moveaxis(table[idx], -1, 0)

def bias_attention(q, k, v, valid, bias):
    s = jnp.einsum('bnqhd,bnthd->bnhqt', q, k).astype(jnp.float32) * (HEAD_DIM ** -0.5)
    s = s + bias.astype(jnp.float32)[None, None]
    s = jnp.where(valid[None, :, None, None, :], s, NEG_INF)
    p = jax.nn.softmax(s, axis=-1)
    return jnp.einsum('bnhqt,bnthd->bnqhd', p.astype(v.dtype), v)

def conv_ffn(h, prev, w_gate, w_up, conv_w, conv_b, w_down):
    g = h @ w_gate
    u = h @ w_up
    l = g.shape[1]
    gp = jnp.concatenate([prev.astype(g.dtype), g], axis=1)
    gc = conv_b
    for i in range(CONV_W):
        gc = gc + conv_w[i] * gp[:, i:i + l]
    y = (jax.nn.gelu(gc) * u) @ w_down
    return y, gp[:, -(CONV_W - 1):]

def mixer_prompt(hn, w_in, sinks, rel_table):
    b, l, _ = hn.shape
    nc = l // CHUNK
    qa, ka, va, ga, qb, kb, vb, qc, kc, vc = split_proj(hn @ w_in)
    pos = jnp.arange(l)
    qa = rotary(qa, pos)
    ka = rotary(ka, pos) * (HEAD_DIM ** -0.5)
    oa, s_ret = retention_prompt(qa, ka, va)
    oa = retention_out(oa, ga).reshape(b, l, H_RET * HEAD_DIM)
    qbc = qb.reshape(b, nc, CHUNK, KV_SWA, G_SWA, HEAD_DIM)
    ob = sink_attention(qbc, band(kb, SWA_PREV_CHUNKS), band(vb, SWA_PREV_CHUNKS),
                        band_valid(nc, SWA_PREV_CHUNKS), sinks).reshape(b, l, H_SWA * HEAD_DIM)
    qcc = qc.reshape(b, nc, CHUNK, H_CA, HEAD_DIM)
    bias = rel_bias_matrix(rel_table, CHUNK, CA_ROWS, (CA_PREV_CHUNKS + 1) * CHUNK)
    oc = bias_attention(qcc, band(kc, CA_PREV_CHUNKS), band(vc, CA_PREV_CHUNKS),
                        band_valid(nc, CA_PREV_CHUNKS), bias).reshape(b, l, H_CA * HEAD_DIM)
    mixed = jnp.concatenate([oa, ob, oc], axis=-1)
    rs = min(SWA_ROWS, l)
    rc = min(CA_ROWS, l)
    return mixed, kb[:, -rs:], vb[:, -rs:], kc[:, -rc:], vc[:, -rc:], s_ret.astype(hn.dtype)

def mixer_sample(hn, ck_b, cv_b, ck_c, cv_c, s_ret, w_in, sinks, rel_table):
    b, t, _ = hn.shape
    qa, ka, va, ga, qb, kb, vb, qc, kc, vc = split_proj(hn @ w_in)
    pos = PAST_LEN + jnp.arange(t)
    qa = rotary(qa, pos)
    ka = rotary(ka, pos) * (HEAD_DIM ** -0.5)
    oa, s_new = retention_block(qa.astype(jnp.float32), ka.astype(jnp.float32),
                                va.astype(jnp.float32), s_ret.astype(jnp.float32))
    oa = retention_out(oa, ga).reshape(b, t, H_RET * HEAD_DIM)
    kb_all = jnp.concatenate([ck_b.astype(kb.dtype), kb], axis=1)
    vb_all = jnp.concatenate([cv_b.astype(vb.dtype), vb], axis=1)
    ob = sink_attention(qb.reshape(b, 1, t, KV_SWA, G_SWA, HEAD_DIM), kb_all[:, None], vb_all[:, None],
                        jnp.ones((1, kb_all.shape[1]), bool), sinks).reshape(b, t, H_SWA * HEAD_DIM)
    lc = ck_c.shape[1]
    kc_all = jnp.concatenate([ck_c.astype(kc.dtype), kc], axis=1)
    vc_all = jnp.concatenate([cv_c.astype(vc.dtype), vc], axis=1)
    bias = rel_bias_matrix(rel_table, t, lc, lc + t)
    oc = bias_attention(qc[:, None], kc_all[:, None], vc_all[:, None],
                        jnp.ones((1, lc + t), bool), bias).reshape(b, t, H_CA * HEAD_DIM)
    mixed = jnp.concatenate([oa, ob, oc], axis=-1)
    rs = ck_b.shape[1]
    return (mixed, kb_all[:, -rs:], vb_all[:, -rs:], kc_all[:, -lc:], vc_all[:, -lc:],
            s_new.astype(s_ret.dtype))

def setup_inputs(seed: int = 0) -> dict:
    key = jax.random.key(seed)
    ks = jax.random.split(key, 24)
    f32 = jnp.float32

    def nrm(k, shape, scale):
        return jax.random.normal(k, shape, f32) * scale

    swa_rows = min(SWA_ROWS, PAST_LEN)
    ca_rows = min(CA_ROWS, PAST_LEN)
    return {
        "x_prompt": nrm(ks[0], (BATCH, SEQ, D_MODEL), 1.0),
        "x_sample": nrm(ks[1], (DEC_BATCH, DEC_SEQ, D_MODEL), 1.0),
        "cache_swa_k": nrm(ks[2], (DEPTH, DEC_BATCH, swa_rows, KV_SWA, HEAD_DIM), 1.0),
        "cache_swa_v": nrm(ks[3], (DEPTH, DEC_BATCH, swa_rows, KV_SWA, HEAD_DIM), 1.0),
        "cache_ca_k": nrm(ks[4], (DEPTH, DEC_BATCH, ca_rows, H_CA, HEAD_DIM), 1.0),
        "cache_ca_v": nrm(ks[5], (DEPTH, DEC_BATCH, ca_rows, H_CA, HEAD_DIM), 1.0),
        "state_ret": nrm(ks[6], (DEPTH, DEC_BATCH, H_RET, HEAD_DIM, HEAD_DIM), 1.0),
        "state_ffn_conv": nrm(ks[7], (DEPTH, DEC_BATCH, CONV_W - 1, D_FF), 1.0),
        "w_in": nrm(ks[8], (DEPTH, D_MODEL, IN_COLS), D_MODEL ** -0.5),
        "w_out": nrm(ks[9], (DEPTH, MIX_WIDTH, D_MODEL), MIX_WIDTH ** -0.5),
        "attn_sinks": nrm(ks[10], (DEPTH, H_SWA), 0.5),
        "rel_bias_table": nrm(ks[11], (DEPTH, N_REL, H_CA), 0.1),
        "norm_mix": 1.0 + nrm(ks[12], (DEPTH, D_MODEL), 0.01),
        "norm_ffn": 1.0 + nrm(ks[13], (DEPTH, D_MODEL), 0.01),
        "w_gate": nrm(ks[14], (DEPTH, D_MODEL, D_FF), D_MODEL ** -0.5),
        "w_up": nrm(ks[15], (DEPTH, D_MODEL, D_FF), D_MODEL ** -0.5),
        "conv_w": nrm(ks[16], (DEPTH, CONV_W, D_FF), CONV_W ** -0.5),
        "conv_b": nrm(ks[17], (DEPTH, D_FF), 0.01),
        "w_down": nrm(ks[18], (DEPTH, D_FF, D_MODEL), D_FF ** -0.5),
        "norm_final": 1.0 + nrm(ks[19], (D_MODEL,), 0.01),
    }

def reference(x_prompt, x_sample, cache_swa_k, cache_swa_v, cache_ca_k, cache_ca_v, state_ret,
              state_ffn_conv, w_in, w_out, attn_sinks, rel_bias_table, norm_mix, norm_ffn, w_gate,
              w_up, conv_w, conv_b, w_down, norm_final):
    hp = x_prompt
    hs = x_sample
    sp = [[] for _ in range(6)]
    ss = [[] for _ in range(6)]
    for l in range(DEPTH):
        sinks_l = attn_sinks[l].reshape(KV_SWA, G_SWA)
        mp, kbp, vbp, kcp, vcp, srp = mixer_prompt(rms_norm(hp, norm_mix[l]), w_in[l], sinks_l,
                                                   rel_bias_table[l])
        hp = hp + mp @ w_out[l]
        zero_conv = jnp.zeros((hp.shape[0], CONV_W - 1, D_FF), hp.dtype)
        fp, cvp = conv_ffn(rms_norm(hp, norm_ffn[l]), zero_conv, w_gate[l], w_up[l], conv_w[l],
                           conv_b[l], w_down[l])
        hp = hp + fp
        ms, kbs, vbs, kcs, vcs, srs = mixer_sample(rms_norm(hs, norm_mix[l]), cache_swa_k[l], cache_swa_v[l],
                                                   cache_ca_k[l], cache_ca_v[l], state_ret[l], w_in[l],
                                                   sinks_l, rel_bias_table[l])
        hs = hs + ms @ w_out[l]
        fs, cvs = conv_ffn(rms_norm(hs, norm_ffn[l]), state_ffn_conv[l], w_gate[l], w_up[l], conv_w[l],
                           conv_b[l], w_down[l])
        hs = hs + fs
        for lst, val in zip(sp, (kbp, vbp, kcp, vcp, srp, cvp)):
            lst.append(val)
        for lst, val in zip(ss, (kbs, vbs, kcs, vcs, srs, cvs)):
            lst.append(val)
    y_prompt = rms_norm(hp, norm_final)
    y_sample = rms_norm(hs, norm_final)
    swa_k_p, swa_v_p, ca_k_p, ca_v_p, ret_p, conv_p = [jnp.stack(v, axis=0) for v in sp]
    swa_k_s, swa_v_s, ca_k_s, ca_v_s, ret_s, conv_s = [jnp.stack(v, axis=0) for v in ss]
    return (y_prompt, y_sample, swa_k_p, swa_v_p, ca_k_p, ca_v_p, ret_p, conv_p,
            swa_k_s, swa_v_s, ca_k_s, ca_v_s, ret_s, conv_s)


_drawn_inputs = setup_inputs


def setup_inputs(seed=0):
    import zlib

    import numpy as np

    out = dict(_drawn_inputs(seed))
    spreads = {}
    factors = {'attn_sinks': 64.0,
     'rel_bias_table': 4.815,
     'norm_mix': 3.362,
     'norm_ffn': 4.892,
     'conv_b': 7.32,
     'norm_final': 32.353}
    for name, (base, spread) in spreads.items():
        noise = np.random.default_rng([zlib.crc32(name.encode()), seed]).standard_normal(out[name].shape)
        drawn = base * np.exp(spread * noise) if base else spread * noise
        out[name] = jnp.asarray(drawn.astype(out[name].dtype))
    for name, factor in factors.items():
        out[name] = (out[name] * factor).astype(out[name].dtype)
    return out
```

```python
import concourse.bass as bass
from concourse import mybir
from contextlib import ExitStack

F32 = mybir.dt.float32
F32R = mybir.dt.float32r
ALU = mybir.AluOpType
ACT = mybir.ActivationFunctionType
AX = mybir.AxisListType

DEPTH, D_MODEL, D_FF, HEAD_DIM = 2, 1024, 2816, 64
SEQ, STREAMS, STEP = 512, 8, 16
P = 128
PROMPT_BLOCKS = SEQ // P
BLOCKS = PROMPT_BLOCKS + 1
SAMPLE = PROMPT_BLOCKS
FRAMES = SEQ + STREAMS * STEP
HALF = FRAMES // 2
HALF_PROMPT, HALF_SAMPLE = SEQ // 2, STREAMS * STEP // 2
KT = D_MODEL // P
H_RET, H_SWA, KV_SWA, G_SWA, H_CA = 6, 6, 2, 3, 4
SWA_CACHE, CA_CACHE = 128, 512
SCALE = HEAD_DIM ** -0.5
NEG_INF = -1e30
EPS = 1e-6
REL_PAD = 399
REL_LEN = REL_PAD + 257
SWA_ROWS = H_SWA * STEP

IN_TILES = 23
TOKEN_SLOT = {**{u: u for u in range(12)}, 16: 12, 21: 13, 22: 14}
FEATURE_SLOT = {12: 0, 13: 1, 14: 2, 15: 3, 17: 4, 18: 5, 19: 6, 20: 7}
TOKEN_TILES = sorted(TOKEN_SLOT)
RET_Q, RET_K, RET_V, RET_G, SWA_V, CA_V = 0, 3, 6, 9, 12, 13
SWA_OUT, CA_OUT, RET_OUT = 0, 3, 6
SWA_Q, SWA_K, CA_Q, CA_K = 0, 3, 4, 6
TOKEN_SLOTS = 15

FFN_HALVES = 2
FF_TILES = D_FF // P
FF_HALF = FF_TILES // FFN_HALVES
DOWN_SPLIT = (6, 5)
CONV_ROW = 2 + SEQ
CONV_STREAM = 2 + STEP
CONV_LEN = CONV_ROW + STREAMS * CONV_STREAM
CONV_OUT = CONV_LEN - 2

OUT_UNIT = IN_TILES + 1
FFN_UNIT = OUT_UNIT + KT
UNITS_PER_FFN_HALF = 2 * FF_HALF + 2 * KT
UNITS = FFN_UNIT + FFN_HALVES * UNITS_PER_FFN_HALF
SLOT_USES = (UNITS // 2, UNITS // 2 - 1)

_C = {}
_n = 0
for _name, _w in (("ident", P), ("ones", P), ("flip", P), ("flip16", P), ("cos", BLOCKS * HEAD_DIM),
                  ("sin", BLOCKS * HEAD_DIM), ("decay", 2 * 12), ("causal", P), ("causal_sample", P),
                  ("window", 2 * P), ("stream", STREAMS), ("block_decay", 3), ("eps", 1)):
    _C[_name] = (_n, _n + _w)
    _n += _w
N_CONST = _n


CREDIT = 1


class Signal:

    def __init__(self, sem, keys):
        self.sem, self.keys = sem, list(keys)
        self.place = {k: n + 1 for n, k in enumerate(self.keys)}
        self.sent = 0

    def done(self, instruction, key):
        assert self.keys[self.sent] == key, (self.keys[self.sent], key)
        self.sent += 1
        return instruction.then_inc(self.sem, 1)

    def wait(self, engine, layer, key):
        engine.wait_ge(self.sem, layer * len(self.keys) + self.place[key])


def build(nc, x_in, consts, w_in, w_out, w_gu, w_down, gains, gain_final, conv_par, sinks, sinks_rows, rel, swa_kt,
          swa_v, ca_kt, ca_v, ret_state, conv_state, y_out, feat_out, tokv_out, ret_p_out, ret_s_out, conv_out,
          swa_kt_copy, swa_v_copy, ca_kt_copy, ca_v_copy):
    ctx = ExitStack()
    with ctx:
        def sb(name, shape, dt=F32, scope=ctx):
            return scope.enter_context(nc.sbuf_tensor(name, shape, dt))

        def sem(name):
            return ctx.enter_context(nc.semaphore(name))

        def signal(name, keys):
            return Signal(sem(name), keys)

        X = sb("X", [P, KT, FRAMES])
        RAW = sb("RAW", [P, 2, KT * P])
        WH = sb("WH", [P, 2, KT * P], F32R)
        WL = sb("WL", [P, 2, KT * P], F32R)
        CONST = sb("CONST", [P, N_CONST])
        GAIN = sb("GAIN", [P, DEPTH, 2, KT])
        GAINF = sb("GAINF", [P, KT])
        CONVP = sb("CONVP", [P, DEPTH, FF_TILES, 4])
        SINK = sb("SINK", [P, DEPTH, H_SWA])
        NSINK = sb("NSINK", [P, DEPTH, H_SWA])
        SINKR = sb("SINKR", [P, DEPTH])
        NSINKR = sb("NSINKR", [P, DEPTH])
        SM = sb("SM", [P, 3, 5, 8])
        MEAN = sb("MEAN", [P, H_RET])
        VAR = sb("VAR", [P, BLOCKS, H_RET])
        with ExitStack() as under:
            PC = sb("PC", [P, 2048], scope=under)
            PS = sb("PS", [P, 1536], scope=under)
            PTC = sb("PTC", [P, 2048], scope=under)
            PTS = sb("PTS", [P, 1536], scope=under)
            AR = sb("AR", [P, 2 * 768], scope=under)
            ZS = sb("ZS", [P, STREAMS, P], scope=under)
            ZC = sb("ZC", [P, 4, P], scope=under)
        XNH = sb("XNH", [P, KT, FRAMES], F32R)
        XNL = sb("XNL", [P, KT, FRAMES], F32R)
        with ExitStack() as under:
            SQ = sb("SQ", [P, FRAMES], scope=under)
            ACC = sb("ACC", [P, FRAMES], scope=under)
            RS = sb("RS", [P, FRAMES], scope=under)
            FT = sb("FT", [P, 2, FRAMES], scope=under)
        CAK = sb("CAK", [P, 2, 2, CA_CACHE])
        CAV = sb("CAV", [P, 2, 4, 2 * P])
        with ExitStack() as ffn:
            YH = sb("YH", [P, FF_HALF, FRAMES], F32R, scope=ffn)
            YL = sb("YL", [P, FF_HALF, FRAMES], F32R, scope=ffn)
            GP = sb("GP", [P, CONV_LEN], scope=ffn)
            CT = sb("CT", [P, CONV_OUT], scope=ffn)
            UT = sb("UT", [P, FRAMES], scope=ffn)
            YT = sb("YT", [P, FRAMES], scope=ffn)
            HIST = sb("HIST", [P, FF_TILES, STREAMS, 2], scope=ffn)
            TAIL = sb("TAIL", [P, FF_TILES, 2 + 2 * STREAMS], scope=ffn)
        T = sb("T", [P, BLOCKS, TOKEN_SLOTS, P])
        F = sb("F", [P, 8, FRAMES])
        SP = sb("SP", [P, PROMPT_BLOCKS, 3, P])
        ST = sb("ST", [P, 4, H_RET, HEAD_DIM])
        TAB = sb("TAB", [P, H_CA, CA_CACHE])
        STAB = sb("STAB", [P, CA_CACHE + STEP])
        MS = sb("MS", [P, 5, P])
        CO = sb("CO", [P, 4, P])
        with ExitStack() as under:
            SWK = sb("SWK", [P, STREAMS, P], scope=under)
            SWV = sb("SWV", [P, STREAMS, P], scope=under)
        QKT = sb("QKT", [P, 6, FRAMES])
        PSUM = ctx.enter_context(nc.psum_tensor("PSUM", [P, 8, 512], F32))

        def const(name):
            return CONST[:, _C[name][0]:_C[name][1]]

        IDENT, ONES, FLIP, FLIP16 = const("ident"), const("ones"), const("flip"), const("flip16")
        WINDOW = const("window")

        raw_loaded = [sem(f"raw_loaded{s}") for s in range(2)]
        hi_ready = [sem(f"hi_ready{s}") for s in range(2)]
        lo_ready = [sem(f"lo_ready{s}") for s in range(2)]
        unit_used = [sem(f"unit_used{s}") for s in range(2)]
        const_loaded, x_loaded, once_loaded = sem("const_loaded"), sem("x_loaded"), sem("once_loaded")
        ONCE = 16 * (4 + DEPTH * H_SWA)
        states_loaded, rel_loaded, rel_rows_loaded = sem("states_loaded"), sem("rel_loaded"), sem("rel_rows_loaded")
        swa_loaded = sem("swa_loaded")
        cak_loaded = [sem(f"cak_loaded{s}") for s in range(2)]
        cav_loaded = [sem(f"cav_loaded{s}") for s in range(2)]
        hist_loaded = sem("hist_loaded")
        copied, attention_stored, tails_stored, y_stored = (sem("copied"), sem("attention_stored"),
                                                            sem("tails_stored"), sem("y_stored"))
        STORES = 5

        NORMS = ("mix", "ffn")
        squares_step = signal("squares_step", [(n, k) for n in NORMS for k in range(2 * KT - 1)])
        column_sums = signal("column_sums", NORMS)
        root_ready = signal("root_ready", NORMS)
        rstd_ready = signal("rstd_ready", NORMS)

        normed_hi = signal("normed_hi", [(n, k) for n in NORMS for k in range(KT)])
        normed_lo = signal("normed_lo", [(n, k) for n in NORMS for k in range(KT)])
        residual = sem("residual")
        RESIDUALS = KT * (1 + FFN_HALVES)

        in_copied = signal("in_copied", range(IN_TILES))
        turned = signal("turned", TOKEN_TILES)
        GATE_TILES = [u for u in TOKEN_TILES if RET_G <= TOKEN_SLOT[u] < SWA_V]
        gates_ready = signal("gates_ready", GATE_TILES)
        token_ready = signal("token_ready", [u for u in TOKEN_TILES if u not in GATE_TILES])
        rotary_step = signal("rotary_step", [(b, s) for b in range(BLOCKS) for s in range(5)])
        zeroed = signal("zeroed", ["retention", "new rows", "queries"])

        jobs, taker = [], {}

        def job(key, engine):
            jobs.append(key)
            taker[key] = engine

        for s in range(6):
            job(("turn qk", s), "dve" if s % 2 else "act")
        for a in range(2):
            job(("turn qk sample", a), "dve")
        for i in range(PROMPT_BLOCKS):
            for a in range(2):
                job(("ret scores", i, a), "dve")
            job(("ret state", i), "dve")
            job(("ret out", i), "act")
        for a in range(2):
            job(("ret scores", SAMPLE, a), "dve")
        job(("ret out", SAMPLE), "act")
        for a in range(3):
            job(("ret state sample", a), "dve")
        for h in range(H_CA):
            job(("bias", h), "dve")
        for a in range(2):
            job(("bias rows", a), "dve")

        def score_jobs(unit):
            kind, i = unit
            if kind == "swa":
                return [("swa scores", i, kv, g) for g in (0, 2) for kv in range(KV_SWA)]
            if kind == "ca":
                return [("ca scores", i, h) for h in range(H_CA)]
            if kind == "swa sample":
                return [("swas scores", a) for a in range(3)]
            return [("cas scores", i, a) for a in range(2)]

        def turn_jobs(unit):
            kind, i = unit
            if kind == "swa":
                return [("swa turn", i, g) for g in range(G_SWA)]
            if kind == "ca":
                return [("ca turn", i, h) for h in range(H_CA)]
            if kind == "swa sample":
                return [("swas turn", a) for a in range(4)]
            return [("cas turn", i, a) for a in range(2)]

        def out_jobs(unit):
            kind, i = unit
            if kind == "swa sample":
                return [("swas out", a) for a in range(2)]
            return [({"swa": "swa out", "ca": "ca out", "ca sample": "cas out"}[kind], i)]

        ATT_UNITS = [("ca", 0), ("swa", 0), ("ca", 1), ("swa", 1), ("ca sample", 0), ("ca sample", 1), ("swa", 2),
                     ("ca", 2), ("swa", 3), ("ca sample", 2), ("ca sample", 3), ("swa sample", 0), ("ca", 3)]
        N_UNITS = len(ATT_UNITS)
        for u in ATT_UNITS[:2]:
            for k in score_jobs(u):
                job(k, "dve")
        for n, u in enumerate(ATT_UNITS):
            for k in turn_jobs(u):
                job(k, "act")
            for v in ATT_UNITS[n + 2:n + 3]:
                for k in score_jobs(v):
                    job(k, "dve")
            for k in out_jobs(u):
                job(k, "dve")
        job(("cas back",), "dve")
        MIX_JOBS = [(b, a) for b in range(BLOCKS) for a in range(2 if b < SAMPLE else 1)]
        for b, a in MIX_JOBS:
            job(("mix", b, a), "dve")

        order = {k: n for n, k in enumerate(jobs)}
        att_done = signal("att_done", jobs)
        out_dve = signal("out_dve", [k for k in jobs if taker[k] == "dve"])
        out_act = signal("out_act", [k for k in jobs if taker[k] == "act"])
        mixed_hi = signal("mixed_hi", MIX_JOBS + ["sample"])
        mixed_sample_lo = signal("mixed_sample_lo", ["sample"])

        def taken(key):
            return {"dve": out_dve, "act": out_act}[taker[key]]

        def bank(key, width=512):
            return PSUM[:, order[key] % 8, 0:width]

        sinks_negated = sem("sinks_negated")
        row_max = signal("row_max", ATT_UNITS)
        shift_ready = signal("shift_ready", [u for u in ATT_UNITS if u[0].startswith("swa")])
        shifted = signal("shifted", ["swa sample"])
        EXPS = {"swa": H_SWA, "ca": H_CA, "swa sample": 1, "ca sample": 1}
        exp_done = signal("exp_done", [(u, h) for u in ATT_UNITS for h in range(EXPS[u[0]])])
        sink_diff = signal("sink_diff", [u for u in ATT_UNITS if u[0] == "swa"])
        sink_exp = signal("sink_exp", [u for u in ATT_UNITS if u[0].startswith("swa")])
        row_sum = signal("row_sum", ["swa sample"])
        denominator = signal("denominator", [u for u in ATT_UNITS if u[0].startswith("swa")])
        inverse = signal("inverse", ATT_UNITS)
        probs_scaled = signal("probs_scaled", [u for u in ATT_UNITS if u[0].endswith("sample")])
        state_sum = signal("state_sum", list(range(PROMPT_BLOCKS)) + [("s", a) for a in range(3)])
        ret_stat = signal("ret_stat", [(b, s) for b in range(BLOCKS) for s in range(5)]
                          + ["variance", "inverse", "scaled", "gated"])
        ret_root = signal("ret_root", ["root"])
        states_zeroed = signal("states_zeroed", ["states"])
        spread_q = signal("spread_q", ["queries"])
        spread_k = signal("spread_k", range(H_RET))
        k_used = signal("k_used", range(0, H_RET - 2, 2))
        queries_spread = signal("queries_spread", ["queries"])

        pool_passed, sync_passed = sem("pool_passed"), sem("sync_passed")
        pads_zeroed, hist_placed = sem("pads_zeroed"), sem("hist_placed")
        gate_copied = sem("gate_copied")
        tails_kept = sem("tails_kept")
        tap_done, gelu_done, up_copied = sem("tap_done"), sem("gelu_done"), sem("up_copied")
        conv_step = sem("conv_step")
        product_done = sem("product_done")
        y_hi, y_lo = sem("y_hi"), sem("y_lo")
        final_ready = sem("final_ready")

        block = ctx.enter_context(nc.Block())

        def halves(ap):
            return ap.rearrange("p (a n) -> p a n", a=2)

        def unit_use(l, n, extra=0):
            return l * SLOT_USES[n % 2] + n // 2 + extra - int(n % 2 == 1 and n > IN_TILES)

        def product_wait(engine, l, n, extra=0):
            engine.wait_ge(unit_used[n % 2], CREDIT + unit_use(l, n, extra) + 1)

        FFN_EXTRA = UNITS_PER_FFN_HALF // 2
        DOWN_UNIT = FFN_UNIT + 2 * FF_HALF

        def block_cols(ap, b):
            if b < SAMPLE:
                start = (b // 2) * HALF + (b % 2) * P
                return ap[:, start:start + P]
            return halves(ap)[:, :, HALF_PROMPT:HALF]

        def mixed_cols(ap, b, first, n):
            if b < SAMPLE:
                start = (b // 2) * HALF + (b % 2) * P
                return ap[:, first:first + n, start:start + P]
            return ap[:, first:first + n, :].rearrange("p k (a n) -> p k a n", a=2)[:, :, :, HALF_PROMPT:]

        def mixed_src(ap, b):
            return ap if b < SAMPLE else ap.rearrange("p t (a n) -> p t a n", a=2)

        def conv_par_of(l, t):
            return lambda c: CONVP[:, bass.ds(l, 1), bass.ds(t, 1), c]

        def heads(ap):
            return ap.rearrange("p s (h d) -> p (s h) d", d=HEAD_DIM)

        def small(u, what, n, rows=P):
            return SM[0:rows, ATT_UNITS.index(u) % 3, ("shift", "sum", "sink", "den", "inv").index(what), 0:n]

        def spread(ap, shape):
            return ap.rearrange("p (h o) -> p h o", o=1).to_broadcast(shape)

        def swa_keys(i):
            return (2, 0) if i else (1, P)

        QS = AR[:, 0:STREAMS * SWA_ROWS].rearrange("p (b r) -> p b r", b=STREAMS)
        QC = AR[:, STREAMS * SWA_ROWS:STREAMS * SWA_ROWS + 512].rearrange("p (b a r) -> p b a r", b=STREAMS, a=2)
        PS_ROWS = PS[0:SWA_ROWS, 0:STREAMS * (SWA_CACHE + STEP)].rearrange("p (b n) -> p b n", b=STREAMS)
        CA_WIDTH = CA_CACHE + STEP

        @block.sync
        def _(sp):
            sp.dma_start(CONST[:, :], consts).then_inc(const_loaded, 16)
            sp.dma_start(X[:, :, :], x_in).then_inc(x_loaded, 16)
            sp.dma_start(GAINF[:, :], gain_final).then_inc(once_loaded, 16)
            sp.dma_start(GAIN[:, :, :, :], gains).then_inc(once_loaded, 16)
            sp.dma_start(CONVP[:, :, :, :], conv_par).then_inc(once_loaded, 16)
            sp.dma_start(SINK[:, :, :], bass.AP(tensor=sinks.tensor, offset=sinks.offset,
                                                ap=[[0, P], [1, DEPTH * H_SWA]])).then_inc(once_loaded, 16)
            for n in range(DEPTH):
                for c in range(H_SWA):
                    s_c = sinks_rows[n, c:c + 1]
                    sp.dma_start(SINKR[STEP * c:STEP * (c + 1), n:n + 1],
                                 bass.AP(tensor=s_c.tensor, offset=s_c.offset,
                                         ap=[[0, STEP], [1, 1]])).then_inc(once_loaded, 16)

            def load_unit(l, n, source, extra=0, width=KT * P):
                s = n % 2
                sp.wait_ge(lo_ready[s], CREDIT + unit_use(l, n, extra))
                sp.dma_start(RAW[:, s, 0:width], source).then_inc(raw_loaded[s], 16)

            with sp.Fori(0, DEPTH) as l:
                for u in range(2):
                    load_unit(l, u, w_in[l, u])
                squares_step.wait(sp, l, ("mix", 0))
                sp.wait_ge(residual, l * RESIDUALS + KT)
                sp.dma_start(ST[:, :, :, :], ret_state[l]).then_inc(states_loaded, 16)
                for u in range(2, IN_TILES):
                    load_unit(l, u, w_in[l, u])
                for n in range(2):
                    load_unit(l, OUT_UNIT + n, w_out[l, n])
                product_wait(sp, l, IN_TILES - 1)
                r = rel[l, :, STEP:]
                sp.dma_start(PTC[:, :].rearrange("p (h n) -> p h n", h=H_CA),
                             bass.AP(tensor=r.tensor, offset=r.offset, ap=[[1, P], [REL_LEN, H_CA], [1, CA_CACHE]]))\
                    .then_inc(rel_loaded, 16)
                for b2 in range(2):
                    for h in range(H_CA):
                        r = rel[l, h]
                        row = 64 * b2 + STEP * h
                        sp.dma_start(PS[row:row + STEP, 0:CA_WIDTH],
                                     bass.AP(tensor=r.tensor, offset=r.offset, ap=[[1, STEP], [1, CA_WIDTH]]))\
                            .then_inc(rel_rows_loaded, 16)
                turned.wait(sp, l, TOKEN_TILES[-1])
                in_copied.wait(sp, l, IN_TILES - 1)
                for b in range(2):
                    sp.dma_start(CAK[:, b, :, :], ca_kt[l, b]).then_inc(cak_loaded[b], 16)
                    sp.dma_start(CAV[:, b, :, :], ca_v[l, b]).then_inc(cav_loaded[b], 16)
                att_done.wait(sp, l, ("ret out", SAMPLE))
                sp.dma_start(SWK[:, :, :], swa_kt[l]).then_inc(swa_loaded, 16)
                sp.dma_start(SWV[:, :, :], swa_v[l]).then_inc(swa_loaded, 16)
                for r in range(1, 4):
                    for b2 in range(2):
                        if b2 == 0:
                            att_done.wait(sp, l, ("cas scores", r - 1, 1))
                        sp.dma_start(CAK[:, b2, :, :], ca_kt[l, 2 * r + b2]).then_inc(cak_loaded[b2], 16)
                    for b2 in range(2):
                        if b2 == 0:
                            att_done.wait(sp, l, ("cas out", r - 1))
                        sp.dma_start(CAV[:, b2, :, :], ca_v[l, 2 * r + b2]).then_inc(cav_loaded[b2], 16)
                for n in range(2, KT):
                    load_unit(l, OUT_UNIT + n, w_out[l, n])
                sp.wait_ge(attention_stored, 16 * STORES * (l + 1))
                sp.sem_inc(sync_passed, 1)
                sp.wait_ge(residual, l * RESIDUALS + KT + 1)
                sp.dma_start(HIST[:, :, :, :], conv_state[l]).then_inc(hist_loaded, 16)
                with sp.Fori(0, FFN_HALVES) as h:
                    with sp.Fori(0, FF_HALF) as f:
                        for j in range(2):
                            load_unit(l, FFN_UNIT + j, w_gu[l, h, f, j], extra=h * FFN_EXTRA + f)
                    with sp.Fori(0, KT) as m:
                        for j in range(2):
                            load_unit(l, DOWN_UNIT + j, w_down[l, h, m, j, :, 0:DOWN_SPLIT[j] * P],
                                      extra=h * FFN_EXTRA + m, width=DOWN_SPLIT[j] * P)
            for k in range(KT):
                sp.wait_ge(final_ready, k + 1)
                sp.dma_start(y_out[:, k, :], X[:, k, :]).then_inc(y_stored, 16)
            sp.wait_ge(y_stored, 16 * KT)

        @block.gpsimd
        def _(pool):
            def squares(l, name, first_residual):
                for k in range(KT):
                    pool.wait_ge(residual, first_residual + k + 1 - KT)
                    if k >= 1:
                        squares_step.wait(pool, l, (name, 2 * k - 2))
                    squares_step.done(nc.gpsimd.tensor_tensor((SQ if k else ACC)[:, :], X[:, k, :], X[:, k, :],
                                                              ALU.mult), (name, max(2 * k - 1, 0)))
                    if k:
                        squares_step.wait(pool, l, (name, 2 * k - 1))
                        squares_step.done(nc.gpsimd.tensor_tensor(ACC[:, :], ACC[:, :], SQ[:, :], ALU.add),
                                          (name, 2 * k))



            def rotate(l, b):
                half = HEAD_DIM // 2
                x = heads(T[:, b, RET_Q:RET_V, :])
                a = TAB[:, 0:2, :].rearrange("p h n -> p (h n)")[:, 0:768].rearrange("p (h d) -> p h d", d=HEAD_DIM)

                def table(name, first, n):
                    start = _C[name][0] + b * HEAD_DIM + first
                    return CONST[:, start:start + n].rearrange("p (o d) -> p o d", o=1).to_broadcast([P, 12, n])

                d0 = _C["decay"][0] + 12 * int(b == SAMPLE)
                decay = spread(CONST[:, d0:d0 + 12], [P, 12, HEAD_DIM])
                if b:
                    rotary_step.wait(pool, l, (b - 1, 4))
                rotary_step.done(nc.gpsimd.tensor_tensor(a[:, :, 0:half], x[:, :, half:], table("sin", 0, half),
                                                         ALU.mult), (b, 0))
                rotary_step.done(nc.gpsimd.tensor_tensor(a[:, :, half:], x[:, :, 0:half], table("sin", half, half),
                                                         ALU.mult), (b, 1))
                rotary_step.wait(pool, l, (b, 1))
                rotary_step.done(nc.gpsimd.tensor_tensor(x, x, table("cos", 0, HEAD_DIM), ALU.mult), (b, 2))
                rotary_step.wait(pool, l, (b, 2))
                rotary_step.done(nc.gpsimd.tensor_tensor(x, x, a, ALU.add), (b, 3))
                rotary_step.wait(pool, l, (b, 3))
                rotary_step.done(nc.gpsimd.tensor_tensor(x, x, decay, ALU.mult), (b, 4))

            for s in (tails_kept, product_done):
                nc.gpsimd.sem_inc(s, CREDIT)
            pool.wait_ge(x_loaded, 16)
            pool.wait_ge(const_loaded, 16)
            nc.gpsimd.sem_inc(residual, KT)
            with pool.Fori(0, DEPTH) as l:
                squares(l, "mix", l * RESIDUALS + KT)
                token_ready.wait(pool, l, 5)
                for b in range(BLOCKS):
                    rotate(l, b)
                product_wait(pool, l, IN_TILES - 1)
                pool.sem_inc(pool_passed, 1)
                zeroed.done(nc.gpsimd.memset(PC[:, 0:1024], 0.0), "retention")
                nc.gpsimd.memset(ZS[:, :, :], 0.0)
                zeroed.done(nc.gpsimd.memset(ZC[:, :, :], 0.0), "new rows")
                out_dve.wait(pool, l, ("ret state", PROMPT_BLOCKS - 1))
                in_copied.wait(pool, l, IN_TILES - 1)
                token_ready.wait(pool, l, TOKEN_TILES[-1])
                pool.dma_start(feat_out[l], F[:, :, :]).then_inc(attention_stored, 16)
                pool.dma_start(tokv_out[l], T[:, :, SWA_V:, :]).then_inc(attention_stored, 16)
                for h2 in range(2):
                    rows = slice(64 * h2, 64 * h2 + 64)
                    pool.dma_start(ret_p_out[l, rows], SP[rows, PROMPT_BLOCKS - 1, :, rows])\
                        .then_inc(attention_stored, 16)
                att_done.wait(pool, l, ("ret out", SAMPLE))
                pool.sem_inc(pool_passed, 1)
                zeroed.done(nc.gpsimd.memset(AR[:, :], 0.0), "queries")
                out_dve.wait(pool, l, ("ret state sample", 2))
                pool.dma_start(ret_s_out[l], ST[:, :, :, :]).then_inc(attention_stored, 16)
                squares(l, "ffn", l * RESIDUALS + 2 * KT)
                pool.wait_ge(hist_loaded, 16 * (l + 1))
                pool.sem_inc(pool_passed, 1)
                nc.gpsimd.memset(GP[:, 0:2], 0.0).then_inc(pads_zeroed, 1)
                streams = GP[:, CONV_ROW:].rearrange("p (b t) -> p b t", t=CONV_STREAM)
                def ffn_tile(t):
                    n = l * FF_TILES + t
                    pool.wait_ge(conv_step, CREDIT + 2 * n)
                    nc.gpsimd.tensor_copy(streams[:, :, 0:2], HIST[:, t, :, :]).then_inc(hist_placed, 1)
                    pool.wait_ge(gate_copied, CREDIT + 2 * n + 2)
                    nc.gpsimd.tensor_copy(TAIL[:, t, 0:2], GP[:, SEQ:CONV_ROW]).then_inc(tails_kept, 1)
                    nc.gpsimd.tensor_copy(TAIL[:, t, 2:].rearrange("p (b t) -> p b t", t=2),
                                          streams[:, :, STEP:CONV_STREAM]).then_inc(tails_kept, 1)
                    pool.wait_ge(y_lo, CREDIT + n)
                    pool.wait_ge(up_copied, CREDIT + n + 1)
                    pool.wait_ge(gelu_done, n + 1)
                    nc.gpsimd.tensor_tensor(halves(YT[:, :])[:, :, 0:HALF_PROMPT], halves(UT[:, :])[:, :, 0:HALF_PROMPT],
                                            halves(CT[:, 0:SEQ]), ALU.mult).then_inc(product_done, 1)
                    ct_streams = bass.AP(tensor=CT[:, :].tensor, offset=CT[:, CONV_ROW:].offset,
                                         ap=[CT[:, :].ap[0], [4 * CONV_STREAM, 2], [CONV_STREAM, 4], [1, STEP]])
                    nc.gpsimd.tensor_tensor(
                        halves(YT[:, :])[:, :, HALF_PROMPT:].rearrange("p a (b t) -> p a b t", t=STEP),
                        halves(UT[:, :])[:, :, HALF_PROMPT:].rearrange("p a (b t) -> p a b t", t=STEP),
                        ct_streams, ALU.mult).then_inc(product_done, 1)
                with pool.Fori(0, STREAMS) as b:
                    for out, src in ((ca_kt_copy, ca_kt), (ca_v_copy, ca_v)):
                        pool.dma_start(out[l, b], src[l, b]).then_inc(copied, 16)
                    for j in range(2):
                        ffn_tile(2 * b + j)
                for out, src in ((swa_kt_copy, swa_kt), (swa_v_copy, swa_v)):
                    pool.dma_start(out[l], src[l]).then_inc(copied, 16)
                with pool.Fori(2 * STREAMS, FF_TILES) as t:
                    ffn_tile(t)
                pool.wait_ge(tails_kept, CREDIT + 2 * FF_TILES * (l + 1))
                pool.dma_start(conv_out[l], TAIL[:, :, :]).then_inc(tails_stored, 16)
                pool.wait_ge(tails_stored, 16 * (l + 1))
            squares_step.sent = 0
            squares(DEPTH, "mix", DEPTH * RESIDUALS + KT)
            pool.wait_ge(copied, 16 * (2 * STREAMS + 2) * DEPTH)
            pool.wait_ge(attention_stored, 16 * STORES * DEPTH)


        @block.scalar
        def _(act):
            def hi(l, n, extra=0, width=KT * P):
                s = n % 2
                use = unit_use(l, n, extra)
                act.wait_ge(raw_loaded[s], 16 * use + 16)
                act.wait_ge(unit_used[s], CREDIT + use)
                nc.scalar.activation(WH[:, s, 0:width], RAW[:, s, 0:width], ACT.Copy).then_inc(hi_ready[s], 1)

            def norm(l, name):
                column_sums.wait(act, l, name)
                root_ready.done(nc.scalar.activation(halves(RS[:, :]), PSUM[:, 4:6, 0:HALF], ACT.Sqrt,
                                                     bias=const("eps"), scale=1.0 / D_MODEL), name)

            def norm_hi(l, name, which, first_residual):
                for k in range(KT):
                    act.wait_ge(residual, first_residual + k + 1 - KT)
                    normed_hi.done(nc.scalar.activation(XNH[:, k, :], X[:, k, :], ACT.Copy,
                                                        scale=GAIN[:, bass.ds(l, 1), which, k:k + 1]
                                                        .rearrange("p a b -> p (a b)")), (name, k))

            def take_turned(l, u):
                turned.wait(act, l, u)
                b = 4 + 2 * (TOKEN_TILES.index(u) % 2)
                slot = TOKEN_SLOT[u]
                ready, function = (gates_ready, ACT.Silu) if u in GATE_TILES else (token_ready, ACT.Copy)
                nc.scalar.activation(T[:, 0:SAMPLE, slot, :],
                                     PSUM[:, b, :].rearrange("p (b n) -> p b n", b=PROMPT_BLOCKS), function)
                ready.done(nc.scalar.activation(T[:, SAMPLE, slot, :], PSUM[:, b + 1, 0:P], function), u)

            def exps(l, u):
                kind, i = u
                if kind == "swa":
                    w0 = swa_keys(i)[1]
                    shift_ready.wait(act, l, u)
                    for h in range(H_SWA):
                        p = PS[:, 256 * h + w0:256 * (h + 1)]
                        exp_done.done(nc.scalar.activation(p, p, ACT.Exp, bias=small(u, "shift", 8)[:, h:h + 1],
                                                           accum_out=small(u, "sum", 8)[:, h:h + 1]), (u, h))
                    sink_diff.wait(act, l, u)
                    sink_exp.done(nc.scalar.activation(small(u, "sink", 6), small(u, "sink", 6), ACT.Exp), u)
                elif kind == "ca":
                    row_max.wait(act, l, u)
                    for h in range(H_CA):
                        p = PC[:, 512 * h:512 * h + P * (i + 1)]
                        exp_done.done(nc.scalar.activation(p, p, ACT.Exp, bias=small(u, "shift", 8)[:, h:h + 1],
                                                           accum_out=small(u, "sum", 8)[:, h:h + 1]), (u, h))
                elif kind == "swa sample":
                    shifted.wait(act, l, "swa sample")
                    exp_done.done(nc.scalar.activation(PS_ROWS, PS_ROWS, ACT.Exp), (u, 0))
                    sink_exp.done(nc.scalar.activation(small(u, "sink", 8, SWA_ROWS), small(u, "shift", 8, SWA_ROWS),
                                                       ACT.Exp, bias=sink_row(l)), u)
                else:
                    row_max.wait(act, l, u)
                    p = PC[:, (i % 2) * CA_WIDTH:(i % 2 + 1) * CA_WIDTH]
                    exp_done.done(nc.scalar.activation(p, p, ACT.Exp, bias=small(u, "shift", 1),
                                                       accum_out=small(u, "sum", 1)), (u, 0))

            def sink_row(l):
                return SINKR[0:SWA_ROWS, bass.ds(l, 1)]

            def take_turns(l, u):
                kind, i = u
                for m, k in enumerate(turn_jobs(u)):
                    att_done.wait(act, l, k)
                    if kind == "swa":
                        count, _ = swa_keys(i)
                        src = bank(k).rearrange("p (h n) -> p h n", h=2)[:, :, P * (2 - count):]
                        dst = PTS[:, 512 * m:512 * (m + 1)].rearrange("p (h n) -> p h n", h=2)[:, :, P * (2 - count):]
                    elif kind == "ca":
                        src, dst = bank(k, P * (i + 1)), PTC[:, 512 * m:512 * m + P * (i + 1)]
                    elif kind == "swa sample":
                        src, dst = bank(k, 4 * SWA_ROWS), PTS[:, 4 * SWA_ROWS * m:4 * SWA_ROWS * (m + 1)]
                    else:
                        start = 640 * (i % 2) + 512 * m
                        w = P if m else 512
                        src, dst = bank(k, w), PTC[:, start:start + w]
                    out_act.done(nc.scalar.activation(dst, src, ACT.Copy), k)

            act.wait_ge(const_loaded, 16)
            act.wait_ge(once_loaded, ONCE)
            with act.Fori(0, DEPTH) as l:
                hi(l, 0)
                norm_hi(l, "mix", 0, l * RESIDUALS + KT)
                hi(l, 1)
                hi(l, 2)
                norm(l, "mix")
                for u in range(IN_TILES):
                    if 2 <= u < IN_TILES - 1:
                        hi(l, u + 1)
                    if u - 2 in TOKEN_SLOT:
                        take_turned(l, u - 2)
                for u in (IN_TILES - 2, IN_TILES - 1):
                    take_turned(l, u)
                for n in range(2):
                    hi(l, OUT_UNIT + n)
                for s in range(0, 6, 2):
                    att_done.wait(act, l, ("turn qk", s))
                    out_act.done(nc.scalar.activation(QKT[:, s, 0:SEQ], bank(("turn qk", s)), ACT.Copy), ("turn qk", s))
                for b in range(BLOCKS):
                    att_done.wait(act, l, ("ret out", b) if b < SAMPLE else ("ret state sample", 2))
                    out_act.done(nc.scalar.activation(T[:, b, RET_OUT:RET_OUT + 3, :],
                                                      bank(("ret out", b), 384).rearrange("p (s n) -> p s n", s=3),
                                                      ACT.Copy), ("ret out", b))
                ret_stat.wait(act, l, "variance")
                ret_root.done(nc.scalar.activation(VAR[:, :, :], VAR[:, :, :], ACT.Sqrt), "root")
                for u in ATT_UNITS[:2]:
                    exps(l, u)
                for n, u in enumerate(ATT_UNITS):
                    take_turns(l, u)
                    for v in ATT_UNITS[n + 2:n + 3]:
                        exps(l, v)
                for b, a in MIX_JOBS:
                    att_done.wait(act, l, ("mix", b, a))
                    n = 4 if b < SAMPLE else 3
                    src = bank(("mix", b, a), n * P).rearrange("p (t n) -> p t n", t=n)
                    mixed_hi.done(nc.scalar.activation(mixed_cols(XNH, b, 4 * a, n), mixed_src(src, b), ACT.Copy),
                                  (b, a))
                out_dve.wait(act, l, ("cas back",))
                mixed_hi.done(nc.scalar.activation(mixed_cols(XNH, SAMPLE, 3, 5), mixed_src(MS[:, :, :], SAMPLE),
                                                   ACT.Copy), "sample")
                for m in range(2, KT + 1):
                    hi(l, OUT_UNIT + m)
                product_wait(act, l, OUT_UNIT + KT - 1)
                norm_hi(l, "ffn", 1, l * RESIDUALS + 2 * KT)
                hi(l, FFN_UNIT + 1)
                norm(l, "ffn")
                for h in range(FFN_HALVES):
                    with act.Fori(0, FF_HALF) as f:
                        extra = h * FFN_EXTRA + f
                        t = h * FF_HALF + f
                        n = l * FF_TILES + t
                        par = conv_par_of(l, t)
                        act.wait_ge(hist_placed, n + 1)
                        act.wait_ge(product_done, CREDIT + 2 * n)
                        act.wait_ge(gate_copied, CREDIT + 2 * n + 2)
                        nc.scalar.activation(CT[:, :], GP[:, 2:], ACT.Copy, scale=par(2)).then_inc(tap_done, 1)
                        hi(l, FFN_UNIT + 2, extra)
                        act.wait_ge(conv_step, CREDIT + 2 * n + 2)
                        nc.scalar.activation(CT[:, :], CT[:, :], ACT.Gelu_apprx_tanh, bias=par(3)).then_inc(gelu_done, 1)
                        hi(l, FFN_UNIT + 3, extra)
                        if h:
                            product_wait(act, l, DOWN_UNIT + 2 * KT - 1)
                        act.wait_ge(product_done, CREDIT + 2 * n + 2)
                        nc.scalar.activation(YH[:, f, :], YT[:, :], ACT.Copy).then_inc(y_hi, 1)
                    with act.Fori(0, KT - 1) as m:
                        for j in range(2):
                            hi(l, DOWN_UNIT + 2 + j, h * FFN_EXTRA + m, DOWN_SPLIT[j] * P)
                    if h < FFN_HALVES - 1:
                        for j in range(2):
                            hi(l, FFN_UNIT + j, FFN_EXTRA)
            column_sums.wait(act, DEPTH, "mix")
            nc.scalar.activation(halves(RS[:, :]), PSUM[:, 0:2, 0:HALF], ACT.Sqrt, bias=const("eps"),
                                 scale=1.0 / D_MODEL).then_inc(root_ready.sem, 1)

        @block.vector
        def _(dve):
            def lo(l, n, extra=0, width=KT * P):
                s = n % 2
                dve.wait_ge(hi_ready[s], unit_use(l, n, extra) + 1)
                nc.vector.tensor_tensor(WL[:, s, 0:width], RAW[:, s, 0:width], WH[:, s, 0:width].bitcast(F32),
                                        ALU.subtract).then_inc(lo_ready[s], 1)

            def reciprocal_root(l, name):
                root_ready.wait(dve, l, name)
                rstd_ready.done(nc.vector.reciprocal(RS[:, :], RS[:, :]), name)

            def norm_lo(l, name, which, first_residual):
                for k in range(KT):
                    dve.wait_ge(residual, first_residual + k + 1 - KT)
                    normed_hi.wait(dve, l, (name, k))
                    normed_lo.done(nc.vector.scalar_tensor_tensor(out=XNL[:, k, :], in0=X[:, k, :],
                                                                  scalar=GAIN[:, bass.ds(l, 1), which, k],
                                                                  in1=XNH[:, k, :].bitcast(F32),
                                                                  op0=ALU.mult, op1=ALU.subtract), (name, k))

            def in_copy(l, u):
                product_wait(dve, l, u)
                if u in TOKEN_SLOT:
                    n = TOKEN_TILES.index(u)
                    if n >= 2:
                        turned.wait(dve, l, TOKEN_TILES[n - 2])
                    out = FT[:, n % 2, :]
                else:
                    out = F[:, FEATURE_SLOT[u], :]
                b, rs = 2 * (u % 2), halves(RS[:, :])
                nc.vector.tensor_tensor(halves(out[:, 0:SEQ]), PSUM[:, b:b + 2, 0:HALF_PROMPT], rs[:, :, 0:HALF_PROMPT],
                                        ALU.mult)
                in_copied.done(nc.vector.tensor_tensor(halves(out[:, SEQ:]), PSUM[:, b:b + 2, HALF_PROMPT:HALF],
                                                       rs[:, :, HALF_PROMPT:], ALU.mult), u)

            def take(l, key, instruction):
                return out_dve.done(instruction, key)

            def mask_scores(l, b, a):
                key = ("ret scores", b, a)
                att_done.wait(dve, l, key)
                if a == 0 and b >= 2:
                    att_done.wait(dve, l, ("ret out", b - 2))
                start = 768 * (b % 2) + 384 * a
                mask = const("causal_sample" if b == SAMPLE else "causal")
                take(l, key, nc.vector.tensor_tensor(
                    AR[:, start:start + 384].rearrange("p (h n) -> p h n", h=3),
                    bank(key, 384).rearrange("p (h n) -> p h n", h=3),
                    mask.rearrange("p (o n) -> p o n", o=1).to_broadcast([P, 3, P]), ALU.mult))

            def prompt_state(l, i):
                key = ("ret state", i)
                att_done.wait(dve, l, key)
                for h2 in range(2):
                    rows, cols = slice(64 * h2, 64 * h2 + 64), slice(64 * h2, 64 * h2 + 64)
                    u = bank(key, 384).rearrange("p (s n) -> p s n", s=3)[rows, :, cols]
                    if i:
                        if h2 == 0:
                            out_dve.wait(dve, l, ("ret state", i - 1))
                        last = nc.vector.tensor_tensor(SP[rows, i, :, cols], u, SP[rows, i - 1, :, cols], ALU.add)
                    else:
                        last = nc.vector.tensor_copy(SP[rows, i, :, cols], u)
                state_sum.done(last, i)
                state_sum.wait(dve, l, i)
                take(l, key, nc.vector.tensor_tensor(SP[:, i, :, :], SP[:, i, :, :],
                                                     spread(const("block_decay"), [P, 3, P]), ALU.mult))

            def statistics(l, b):
                out_act.wait(dve, l, ("ret out", b))
                o = heads(T[:, b, RET_OUT:RET_OUT + 3, :])
                sq = PTS[:, 0:384].rearrange("p (h d) -> p h d", d=HEAD_DIM)
                ret_stat.done(nc.vector.reduce_sum(MEAN[:, :], o, AX.X), (b, 0))
                ret_stat.wait(dve, l, (b, 0))
                ret_stat.done(nc.vector.tensor_scalar(MEAN[:, :], MEAN[:, :], 1.0 / HEAD_DIM, None, ALU.mult), (b, 1))
                ret_stat.wait(dve, l, (b, 1))
                ret_stat.done(nc.vector.tensor_tensor(o, o, spread(MEAN[:, :], [P, H_RET, HEAD_DIM]), ALU.subtract),
                              (b, 2))
                ret_stat.wait(dve, l, (b, 2))
                ret_stat.done(nc.vector.tensor_tensor(sq, o, o, ALU.mult), (b, 3))
                ret_stat.wait(dve, l, (b, 3))
                ret_stat.done(nc.vector.reduce_sum(VAR[:, b, :], sq, AX.X), (b, 4))

            def spread_queries(l):
                zeroed.wait(dve, l, "retention")
                for h2 in range(2):
                    for b2 in range(2):
                        q = QKT[64 * h2:64 * h2 + 64, 0:3, SEQ:].rearrange("p s (a b t) -> p s a b t", b=2, t=STEP)
                        wide = PC[64 * b2:64 * b2 + 64, 0:H_RET * P]                            .rearrange("p (s h a b t) -> p s h a b t", s=3, h=2, b=2, t=STEP)
                        last = nc.vector.tensor_copy(wide[:, :, h2, :, b2, :], q[:, :, :, b2, :])
                spread_q.done(last, "queries")

            def diagonal(ap, n, step, first):
                return bass.AP(tensor=ap.tensor, offset=ap.offset + first, ap=[ap.ap[0], [step, n], [1, STEP]])

            def spread_keys(l, h):
                if h >= 2 and h - 2 in k_used.place:
                    k_used.wait(dve, l, h - 2)
                elif h >= 2:
                    att_done.wait(dve, l, ("ret state sample", (h - 2) // 2))
                k = T[:, SAMPLE, RET_K + h // 2, 64 * (h % 2):64 * (h % 2) + 64]
                spread_k.done(nc.vector.tensor_tensor(
                    PC[:, 1024 + 512 * (h % 2):1536 + 512 * (h % 2)].rearrange("p (b d) -> p b d", b=STREAMS),
                    k.rearrange("p (o d) -> p o d", o=1).to_broadcast([P, STREAMS, HEAD_DIM]),
                    spread(const("stream"), [P, STREAMS, HEAD_DIM]), ALU.mult), h)

            def sample_state(l, a):
                key = ("ret state sample", a)
                att_done.wait(dve, l, key)
                st = ST[:, :, 2 * a:2 * a + 2, :]
                state_sum.done(nc.vector.tensor_tensor(
                    st, bank(key).rearrange("p (h q e) -> p q h e", h=2, q=4), st, ALU.add), ("s", a))
                state_sum.wait(dve, l, ("s", a))
                for h in (2 * a, 2 * a + 1):
                    last = nc.vector.tensor_scalar(ST[:, :, h, :], ST[:, :, h, :],
                                                   (1.0 - 2.0 ** (-5 - h)) ** STEP, None, ALU.mult)
                take(l, key, last)

            def retention_variance(l):
                var = VAR[:, :, :].rearrange("p b h -> p (b h)")
                ret_stat.wait(dve, l, (SAMPLE, 4))
                ret_stat.done(nc.vector.tensor_scalar(var, var, 1.0 / HEAD_DIM, EPS, ALU.mult, ALU.add), "variance")

            def finish_retention(l):
                var = VAR[:, :, :].rearrange("p b h -> p (b h)")
                ret_root.wait(dve, l, "root")
                ret_stat.done(nc.vector.reciprocal(var, var), "inverse")
                ret_stat.wait(dve, l, "inverse")
                for b in range(BLOCKS):
                    o = heads(T[:, b, RET_OUT:RET_OUT + 3, :])
                    last = nc.vector.tensor_tensor(o, o, spread(VAR[:, b, :], [P, H_RET, HEAD_DIM]), ALU.mult)
                ret_stat.done(last, "scaled")
                ret_stat.wait(dve, l, "scaled")
                gates_ready.wait(dve, l, GATE_TILES[-1])
                o = T[:, :, RET_OUT:RET_OUT + 3, :].rearrange("p b s n -> p b (s n)")
                ret_stat.done(nc.vector.tensor_tensor(o, o, T[:, :, RET_G:RET_G + 3, :]
                                                      .rearrange("p b s n -> p b (s n)"), ALU.mult), "gated")

            def place_queries(l):
                zeroed.wait(dve, l, "queries")
                for g in range(G_SWA):
                    for kv in range(KV_SWA):
                        rows = slice(64 * kv, 64 * kv + 64)
                        c = (kv * G_SWA + g) * STEP
                        nc.vector.tensor_copy(QS[rows, :, c:c + STEP],
                                              F[rows, SWA_Q + g, SEQ:].rearrange("p (b t) -> p b t", t=STEP))
                for a in range(2):
                    for h2 in range(2):
                        rows = slice(64 * h2, 64 * h2 + 64)
                        last = nc.vector.tensor_copy(QC[rows, :, a, STEP * h2:STEP * (h2 + 1)],
                                                     F[rows, CA_Q + a, SEQ:].rearrange("p (b t) -> p b t", t=STEP))
                queries_spread.done(last, "queries")

            def take_scores(l, u):
                kind, i = u

                if kind == "swa":
                    count, w0 = swa_keys(i)
                    scores = PS[:, :].rearrange("p (h n) -> p h n", h=H_SWA)[:, :, w0:]
                    for k in score_jobs(u):
                        att_done.wait(dve, l, k)
                        _, _, kv, g = k
                        n = 2 if g == 0 else 1
                        take(l, k, nc.vector.scalar_tensor_tensor(
                            out=scores[:, 2 * g + kv:2 * g + kv + 2 * n - 1:2, :],
                            in0=bank(k, n * 256).rearrange("p (h n) -> p h n", h=n)[:, :, w0:], scalar=SCALE,
                            in1=WINDOW[:, w0:].rearrange("p (o n) -> p o n", o=1).to_broadcast([P, n, 256 - w0]),
                            op0=ALU.mult, op1=ALU.add))
                    out_dve.wait(dve, l, score_jobs(u)[-1])
                    row_max.done(nc.vector.tensor_reduce(small(u, "shift", 6), scores, AX.X, ALU.max, negate=True), u)
                    row_max.wait(dve, l, u)
                    shift_ready.done(nc.vector.tensor_tensor(small(u, "shift", 6), small(u, "shift", 6),
                                                             NSINK[:, bass.ds(l, 1), :].rearrange("p a h -> p (a h)"),
                                                             ALU.min), u)
                    shift_ready.wait(dve, l, u)
                    sink_diff.done(nc.vector.tensor_tensor(small(u, "sink", 6), small(u, "shift", 6),
                                                           SINK[:, bass.ds(l, 1), :].rearrange("p a h -> p (a h)"),
                                                           ALU.add), u)
                elif kind == "ca":
                    w = P * (i + 1)
                    scores = PC[:, :].rearrange("p (h n) -> p h n", h=H_CA)[:, :, 0:w]
                    for h, k in enumerate(score_jobs(u)):
                        att_done.wait(dve, l, k)
                        take(l, k, nc.vector.scalar_tensor_tensor(
                            out=scores[:, h, :], in0=bank(k, w), scalar=SCALE, in1=TAB[:, h, CA_CACHE - w:],
                            op0=ALU.mult, op1=ALU.add))
                    out_dve.wait(dve, l, score_jobs(u)[-1])
                    row_max.done(nc.vector.tensor_reduce(small(u, "shift", 4), scores, AX.X, ALU.max, negate=True), u)
                elif kind == "swa sample":
                    shift = small(u, "shift", 8, SWA_ROWS)
                    for a, k in enumerate(score_jobs(u)):
                        att_done.wait(dve, l, k)
                        m = min(3, STREAMS - 3 * a)
                        take(l, k, nc.vector.tensor_scalar(
                            PS_ROWS[:, 3 * a:3 * a + m, :],
                            bank(k, m * 144)[0:SWA_ROWS].rearrange("p (b n) -> p b n", b=m), SCALE, None, ALU.mult))
                    out_dve.wait(dve, l, score_jobs(u)[-1])
                    row_max.done(nc.vector.tensor_reduce(shift, PS_ROWS, AX.X, ALU.max, negate=True), u)
                    row_max.wait(dve, l, u)
                    shift_ready.done(nc.vector.tensor_scalar(shift, shift, NSINKR[0:SWA_ROWS, bass.ds(l, 1)], None,
                                                             ALU.min), u)
                    shift_ready.wait(dve, l, u)
                    shifted.done(nc.vector.tensor_tensor(PS_ROWS, PS_ROWS, spread(shift, [SWA_ROWS, STREAMS, 144]),
                                                         ALU.add), "swa sample")
                else:
                    p = PC[:, (i % 2) * CA_WIDTH:(i % 2 + 1) * CA_WIDTH]
                    for a, k in enumerate(score_jobs(u)):
                        att_done.wait(dve, l, k)
                        cols = slice(CA_CACHE, CA_WIDTH) if a else slice(0, CA_CACHE)
                        take(l, k, nc.vector.scalar_tensor_tensor(
                            out=p[:, cols], in0=bank(k, STEP if a else CA_CACHE), scalar=SCALE, in1=STAB[:, cols],
                            op0=ALU.mult, op1=ALU.add))
                    out_dve.wait(dve, l, score_jobs(u)[-1])
                    row_max.done(nc.vector.tensor_reduce(small(u, "shift", 1), p, AX.X, ALU.max, negate=True), u)

            def finish_probs(l, u):
                kind, i = u
                exp_done.wait(dve, l, (u, EXPS[kind] - 1))
                if kind == "swa":
                    sink_exp.wait(dve, l, u)
                    denominator.done(nc.vector.tensor_tensor(small(u, "den", 6), small(u, "sum", 6),
                                                             small(u, "sink", 6), ALU.add), u)
                    denominator.wait(dve, l, u)
                    inverse.done(nc.vector.reciprocal(small(u, "inv", 6), small(u, "den", 6)), u)
                elif kind == "ca":
                    inverse.done(nc.vector.reciprocal(small(u, "inv", 4), small(u, "sum", 4)), u)
                elif kind == "swa sample":
                    r = SWA_ROWS
                    row_sum.done(nc.vector.reduce_sum(small(u, "sum", 8, r), PS_ROWS, AX.X), "swa sample")
                    row_sum.wait(dve, l, "swa sample")
                    sink_exp.wait(dve, l, u)
                    denominator.done(nc.vector.tensor_tensor(small(u, "den", 8, r), small(u, "sum", 8, r),
                                                             small(u, "sink", 8, r), ALU.add), u)
                    denominator.wait(dve, l, u)
                    inverse.done(nc.vector.reciprocal(small(u, "inv", 8, r), small(u, "den", 8, r)), u)
                    inverse.wait(dve, l, u)
                    zeroed.wait(dve, l, "new rows")
                    zs = ZS[0:r, :, :].rearrange("p b n -> p (b n)")
                    nc.vector.tensor_tensor(diagonal(zs, STREAMS, P + STEP, 0), PS_ROWS[:, :, SWA_CACHE:],
                                            spread(small(u, "inv", 8, r), [r, STREAMS, STEP]), ALU.mult)
                    probs_scaled.done(nc.vector.tensor_tensor(PS_ROWS[:, :, 0:SWA_CACHE], PS_ROWS[:, :, 0:SWA_CACHE],
                                                              spread(small(u, "inv", 8, r), [r, STREAMS, SWA_CACHE]),
                                                              ALU.mult), u)
                else:
                    p = PC[:, (i % 2) * CA_WIDTH:(i % 2 + 1) * CA_WIDTH]
                    zeroed.wait(dve, l, "new rows")
                    for b2 in range(2):
                        rows, c = slice(64 * b2, 64 * b2 + 64), STEP * (2 * i + b2)
                        last = nc.vector.tensor_copy(ZC[rows, i, c:c + STEP], p[rows, CA_CACHE:])
                    probs_scaled.done(last, u)
                    inverse.done(nc.vector.reciprocal(small(u, "inv", 1), small(u, "sum", 1)), u)

            def take_out(l, u):
                kind, i = u
                for a, k in enumerate(out_jobs(u)):
                    att_done.wait(dve, l, k)
                    if kind in ("swa", "ca"):
                        n = 6 if kind == "swa" else 4
                        slot = SWA_OUT if kind == "swa" else CA_OUT
                        inverse.wait(dve, l, u)
                        take(l, k, nc.vector.tensor_tensor(
                            heads(T[:, i, slot:slot + n // 2, :]), bank(k, n * 64).rearrange("p (h d) -> p h d", h=n),
                            spread(small(u, "inv", n), [P, n, HEAD_DIM]), ALU.mult))
                    elif kind == "swa sample":
                        for kv in range(KV_SWA):
                            rows = slice(64 * kv, 64 * kv + 64)
                            src = bank(k, 384).rearrange("p (b v g t) -> p v g b t", b=4, v=KV_SWA, g=G_SWA)[rows, kv]
                            dst = MS[rows, 0:3, 64 * a:64 * a + 64].rearrange("p g (b t) -> p g b t", t=STEP)
                            last = nc.vector.tensor_copy(dst, src)
                        take(l, k, last)
                    else:
                        inverse.wait(dve, l, u)
                        take(l, k, nc.vector.tensor_scalar(CO[:, i, :], bank(k, P), small(u, "inv", 1), None, ALU.mult))

            for s in (*lo_ready, conv_step, gate_copied, up_copied, y_lo):
                nc.vector.sem_inc(s, CREDIT)
            dve.wait_ge(once_loaded, ONCE)
            dve.wait_ge(const_loaded, 16)
            nc.vector.tensor_scalar(NSINK[:, :, :], SINK[:, :, :], -1.0, None, ALU.mult).then_inc(sinks_negated, 1)
            nc.vector.tensor_scalar(NSINKR[0:SWA_ROWS, :], SINKR[0:SWA_ROWS, :], -1.0, None, ALU.mult)\
                .then_inc(sinks_negated, 1)
            dve.wait_ge(sinks_negated, 2)
            with dve.Fori(0, DEPTH) as l:
                lo(l, 0)
                norm_lo(l, "mix", 0, l * RESIDUALS + KT)
                lo(l, 1)
                lo(l, 2)
                reciprocal_root(l, "mix")
                rstd_ready.wait(dve, l, "mix")
                for u in range(IN_TILES):
                    if 2 <= u < IN_TILES - 1:
                        lo(l, u + 1)
                    in_copy(l, u)
                    if u == RET_V:
                        states_zeroed.done(nc.vector.memset(SP[:, :, :, :], 0.0), "states")
                for n in range(2):
                    lo(l, OUT_UNIT + n)
                for s in range(1, 6, 2):
                    key = ("turn qk", s)
                    att_done.wait(dve, l, key)
                    take(l, key, nc.vector.tensor_copy(QKT[:, s, 0:SEQ], bank(key)))
                for a in range(2):
                    key = ("turn qk sample", a)
                    att_done.wait(dve, l, key)
                    n = 2 if a else 4
                    take(l, key, nc.vector.tensor_copy(QKT[:, 4 * a:4 * a + n, SEQ:],
                                                       bank(key, n * P).rearrange("p (s n) -> p s n", s=n)))
                states_zeroed.wait(dve, l, "states")
                for i in range(PROMPT_BLOCKS):
                    for a in range(2):
                        mask_scores(l, i, a)
                    prompt_state(l, i)
                    if i:
                        statistics(l, i - 1)
                dve.wait_ge(states_loaded, 16 * (l + 1))
                for a in range(2):
                    mask_scores(l, SAMPLE, a)
                spread_queries(l)
                for h in range(2):
                    spread_keys(l, h)
                statistics(l, PROMPT_BLOCKS - 1)
                for a in range(3):
                    for h in (2 * a + 2, 2 * a + 3):
                        if h < H_RET:
                            spread_keys(l, h)
                    sample_state(l, a)
                rotary_step.wait(dve, l, (SAMPLE, 4))
                for h in range(H_CA):
                    key = ("bias", h)
                    att_done.wait(dve, l, key)
                    nc.vector.tensor_copy(TAB[:, h, 0:CA_CACHE - P], bank(key, CA_CACHE - P))
                    take(l, key, nc.vector.tensor_tensor(TAB[:, h, CA_CACHE - P:], bank(key)[:, CA_CACHE - P:],
                                                         WINDOW[:, P:], ALU.add))
                for a in range(2):
                    key = ("bias rows", a)
                    att_done.wait(dve, l, key)
                    cols = slice(CA_CACHE, CA_WIDTH) if a else slice(0, CA_CACHE)
                    take(l, key, nc.vector.tensor_copy(STAB[:, cols], bank(key, STEP if a else CA_CACHE)))
                out_dve.wait(dve, l, ("bias rows", 1))
                statistics(l, SAMPLE)
                retention_variance(l)
                for u in ATT_UNITS[:2]:
                    take_scores(l, u)
                finish_probs(l, ATT_UNITS[0])
                place_queries(l)
                for n, u in enumerate(ATT_UNITS):
                    for v in ATT_UNITS[n + 1:n + 2]:
                        finish_probs(l, v)
                    for v in ATT_UNITS[n + 2:n + 3]:
                        take_scores(l, v)
                    take_out(l, u)
                    if n == 1:
                        finish_retention(l)
                att_done.wait(dve, l, ("cas back",))
                for h2 in range(2):
                    rows = slice(64 * h2, 64 * h2 + 64)
                    src = bank(("cas back",)).rearrange("p (b a h t) -> p h a b t", b=STREAMS, a=2, h=2)[rows, h2]
                    last = nc.vector.tensor_copy(MS[rows, 3:5, :].rearrange("p a (b t) -> p a b t", t=STEP), src)
                take(l, ("cas back",), last)
                out_dve.wait(dve, l, ("cas back",))
                for b, a in MIX_JOBS:
                    key, n = ("mix", b, a), 4 if b < SAMPLE else 3
                    mixed_hi.wait(dve, l, (b, a))
                    src = bank(key, n * P).rearrange("p (t n) -> p t n", t=n)
                    take(l, key, nc.vector.tensor_tensor(mixed_cols(XNL, b, 4 * a, n), mixed_src(src, b),
                                                         mixed_cols(XNH, b, 4 * a, n).bitcast(F32), ALU.subtract))
                mixed_hi.wait(dve, l, "sample")
                mixed_sample_lo.done(nc.vector.tensor_tensor(mixed_cols(XNL, SAMPLE, 3, 5), mixed_src(MS[:, :, :], SAMPLE),
                                                             mixed_cols(XNH, SAMPLE, 3, 5).bitcast(F32), ALU.subtract),
                                     "sample")
                for m in range(KT):
                    product_wait(dve, l, OUT_UNIT + m)
                    b = 2 * (m % 2)
                    nc.vector.tensor_tensor(halves(X[:, m, :]), PSUM[:, b:b + 2, 0:HALF], halves(X[:, m, :]), ALU.add)\
                        .then_inc(residual, 1)
                    if m < KT - 1:
                        lo(l, OUT_UNIT + m + 2)
                norm_lo(l, "ffn", 1, l * RESIDUALS + 2 * KT)
                lo(l, FFN_UNIT + 1)
                reciprocal_root(l, "ffn")
                rs = halves(RS[:, :])
                streams = GP[:, CONV_ROW:].rearrange("p (a b t) -> p a b t", a=2, t=CONV_STREAM)
                for h in range(FFN_HALVES):
                    with dve.Fori(0, FF_HALF) as f:
                        extra = h * FFN_EXTRA + f
                        t = h * FF_HALF + f
                        n = l * FF_TILES + t
                        par = conv_par_of(l, t)
                        rstd_ready.wait(dve, l, "ffn")
                        dve.wait_ge(pads_zeroed, l + 1)
                        product_wait(dve, l, FFN_UNIT, extra)
                        dve.wait_ge(conv_step, CREDIT + 2 * n)
                        dve.wait_ge(tails_kept, CREDIT + 2 * n)
                        nc.vector.tensor_tensor(halves(GP[:, 2:CONV_ROW]), PSUM[:, 0:2, 0:HALF_PROMPT],
                                                rs[:, :, 0:HALF_PROMPT], ALU.mult).then_inc(gate_copied, 1)
                        nc.vector.tensor_tensor(streams[:, :, :, 2:], PSUM[:, 0:2, HALF_PROMPT:HALF]
                                                .rearrange("p a (b t) -> p a b t", t=STEP),
                                                rs[:, :, HALF_PROMPT:].rearrange("p a (b t) -> p a b t", t=STEP),
                                                ALU.mult).then_inc(gate_copied, 1)
                        lo(l, FFN_UNIT + 2, extra)
                        dve.wait_ge(tap_done, n + 1)
                        nc.vector.scalar_tensor_tensor(out=CT[:, :], in0=GP[:, 1:1 + CONV_OUT], scalar=par(1),
                                                       in1=CT[:, :], op0=ALU.mult, op1=ALU.add).then_inc(conv_step, 1)
                        dve.wait_ge(conv_step, CREDIT + 2 * n + 1)
                        nc.vector.scalar_tensor_tensor(out=CT[:, :], in0=GP[:, 0:CONV_OUT], scalar=par(0),
                                                       in1=CT[:, :], op0=ALU.mult, op1=ALU.add).then_inc(conv_step, 1)
                        product_wait(dve, l, FFN_UNIT + 1, extra)
                        dve.wait_ge(product_done, CREDIT + 2 * n)
                        nc.vector.tensor_tensor(halves(UT[:, :]), PSUM[:, 2:4, 0:HALF], rs, ALU.mult)\
                            .then_inc(up_copied, 1)
                        lo(l, FFN_UNIT + 3, extra)
                        dve.wait_ge(y_hi, n + 1)
                        nc.vector.tensor_tensor(YL[:, f, :], YT[:, :], YH[:, f, :].bitcast(F32), ALU.subtract)\
                            .then_inc(y_lo, 1)

                    def add_down(m, parity):
                        product_wait(dve, l, DOWN_UNIT + 1, h * FFN_EXTRA + m)
                        b = 4 + 2 * parity
                        x = X[:, bass.ds(m, 1), :].rearrange("p o (a n) -> p (o a) n", a=2)
                        nc.vector.tensor_tensor(x, PSUM[:, b:b + 2, 0:HALF], x, ALU.add).then_inc(residual, 1)

                    def next_down(m):
                        for j in range(2):
                            lo(l, DOWN_UNIT + 2 + j, h * FFN_EXTRA + m, DOWN_SPLIT[j] * P)

                    with dve.Fori(0, KT // 2 - 1) as m2:
                        for j in range(2):
                            next_down(2 * m2 + j)
                            add_down(2 * m2 + j, j)
                    next_down(KT - 2)
                    add_down(KT - 2, 0)
                    if h < FFN_HALVES - 1:
                        lo(l, FFN_UNIT, FFN_EXTRA)
                    add_down(KT - 1, 1)
                    if h < FFN_HALVES - 1:
                        lo(l, FFN_UNIT + 1, FFN_EXTRA)
            dve.wait_ge(root_ready.sem, 2 * DEPTH + 1)
            nc.vector.reciprocal(RS[:, :], RS[:, :]).then_inc(rstd_ready.sem, 1)
            dve.wait_ge(rstd_ready.sem, 2 * DEPTH + 1)
            for k in range(KT):
                nc.vector.scalar_tensor_tensor(out=X[:, k, :], in0=X[:, k, :], scalar=GAINF[:, k:k + 1],
                                               in1=RS[:, :], op0=ALU.mult, op1=ALU.mult).then_inc(final_ready, 1)

        @block.tensor
        def _(pe):
            def product(l, n, xh, xl, b, extra=0, tiles=KT, first=0, start=True, stop=True, ready=None):
                s = n % 2
                pe.wait_ge(lo_ready[s], CREDIT + unit_use(l, n, extra) + 1)
                for k in range(tiles):
                    if ready:
                        ready(k)
                    for w, x in ((WH, xh), (WH, xl), (WL, xh)):
                        for a in range(2):
                            last = nc.tensor.matmul(
                                PSUM[:, b + a, 0:HALF], w[:, s, P * k:P * (k + 1)],
                                x[:, first + k, HALF * a:HALF * (a + 1)],
                                start=start and k == 0 and w is WH and x is xh,
                                stop=stop and k == tiles - 1 and w is WL)
                last.then_inc(unit_used[s], 1)

            def sum_columns(l, name):
                squares_step.wait(pe, l, (name, 2 * KT - 2))
                for a in range(2):
                    last = nc.tensor.matmul(PSUM[:, 4 + a, 0:HALF], ONES, ACC[:, HALF * a:HALF * (a + 1)],
                                            start=True, stop=True)
                column_sums.done(last, name)

            def turn_tile(l, u):
                n = TOKEN_TILES.index(u)
                in_copied.wait(pe, l, u)
                if n >= 2:
                    before = TOKEN_TILES[n - 2]
                    (gates_ready if before in GATE_TILES else token_ready).wait(pe, l, before)
                b = 4 + 2 * (n % 2)
                for c in range(BLOCKS):
                    last = nc.tensor.transpose(PSUM[:, b + c // 4, P * (c % 4):P * (c % 4 + 1)],
                                               FT[:, n % 2, P * c:P * (c + 1)], IDENT)
                turned.done(last, u)

            def free_bank(l, key):
                n = order[key]
                if n >= 8:
                    taken(jobs[n - 8]).wait(pe, l, jobs[n - 8])

            def mm(out, w, x, start=True, stop=True):
                return nc.tensor.matmul(out, w, x, start=start, stop=stop)

            def retention(l, b):
                sample = b == SAMPLE
                cols = slice(P * b, P * b + P)
                for a in range(2):
                    key = ("ret scores", b, a)
                    free_bank(l, key)
                    rows = slice(64 * a, 64 * a + 64)
                    for c in range(3):
                        last = mm(bank(key)[:, P * c:P * c + P], QKT[rows, 3 + c, cols], QKT[rows, c, cols])
                    att_done.done(last, key)
                ar = AR[:, 768 * (b % 2):768 * (b % 2) + 768]
                if not sample:
                    key = ("ret state", b)
                    free_bank(l, key)
                    for s in range(3):
                        last = mm(bank(key)[:, P * s:P * s + P], T[:, b, RET_K + s, :], T[:, b, RET_V + s, :])
                    att_done.done(last, key)
                key = ("ret out", b)
                free_bank(l, key)
                out_dve.wait(pe, l, ("ret scores", b, 1))
                if b and not sample:
                    out_dve.wait(pe, l, ("ret state", b - 1))
                for h in range(H_RET):
                    rows = slice(64 * (h % 2), 64 * (h % 2) + 64)
                    out = bank(key)[:, 64 * h:64 * h + 64]
                    crossed = b and not sample
                    if crossed and h % 2 == 0:
                        mm(bank(key)[:, 64 * h:64 * h + P], QKT[:, h // 2, cols], SP[:, b - 1, h // 2, :], stop=False)
                    a0 = P * (3 * (h % 2) + h // 2)
                    last = mm(out, ar[:, a0:a0 + P], T[:, b, RET_V + h // 2, rows], start=not crossed,
                              stop=not sample and not (crossed and h % 2 == 0))
                    if sample:
                        if h == 0:
                            spread_q.wait(pe, l, "queries")
                        for q in range(4):
                            last = mm(out[32 * q:32 * q + 32], PC[:, P * h + 32 * q:P * h + 32 * q + 32], ST[:, q, h, :],
                                      start=False)
                att_done.done(last, key)
                if sample:
                    for a in range(3):
                        key = ("ret state sample", a)
                        free_bank(l, key)
                        for c in range(2):
                            h = 2 * a + c
                            spread_k.wait(pe, l, h)
                            for q in range(4):
                                k0 = 1024 + 512 * (h % 2) + P * q
                                last = mm(bank(key)[:, 256 * c + 64 * q:256 * c + 64 * (q + 1)], PC[:, k0:k0 + P],
                                          T[:, SAMPLE, RET_V + h // 2, 64 * (h % 2):64 * (h % 2) + 64])
                            if h in k_used.place:
                                k_used.done(last, h)
                        att_done.done(last, key)

            def scores(l, u):
                kind, i = u
                for a, key in enumerate(score_jobs(u)):
                    free_bank(l, key)
                    if kind == "swa":
                        count, w0 = swa_keys(i)
                        _, _, kv, g = key
                        rows = slice(64 * kv, 64 * kv + 64)
                        for c in range(2 if g == 0 else 1):
                            last = mm(bank(key)[:, 256 * c + w0:256 * c + 256], F[rows, SWA_Q + g + c, P * i:P * i + P],
                                      F[rows, SWA_K, P * (i + 1 - count):P * (i + 1)])
                    elif kind == "ca":
                        rows = slice(64 * (a % 2), 64 * (a % 2) + 64)
                        last = mm(bank(key, P * (i + 1)), F[rows, CA_Q + a // 2, P * i:P * i + P],
                                  F[rows, CA_K + a // 2, 0:P * (i + 1)])
                    elif kind == "swa sample":
                        if a == 0:
                            pe.wait_ge(swa_loaded, 32 * (l + 1))
                            queries_spread.wait(pe, l, "queries")
                        for b in range(3 * a, min(3 * a + 3, STREAMS)):
                            c = 144 * (b - 3 * a)
                            mm(bank(key)[0:SWA_ROWS, c:c + SWA_CACHE], QS[:, b, :], SWK[:, b, :])
                            last = mm(bank(key)[0:SWA_ROWS, c + SWA_CACHE:c + 144], QS[:, b, :],
                                      F[:, SWA_K, SEQ + STEP * b:SEQ + STEP * (b + 1)])
                    else:
                        for b2 in range(2):
                            b = 2 * i + b2
                            if a == 0:
                                pe.wait_ge(cak_loaded[b2], 16 * (4 * l + i + 1))
                            for pair in range(2):
                                r0 = 32 * (2 * b2 + pair)
                                rhs = (F[:, CA_K + pair, SEQ + STEP * b:SEQ + STEP * (b + 1)] if a
                                       else CAK[:, b2, pair, :])
                                last = mm(bank(key, STEP if a else CA_CACHE)[r0:r0 + 32], QC[:, b, pair, :], rhs)
                    att_done.done(last, key)

            def turns(l, u):
                kind, i = u
                for a, key in enumerate(turn_jobs(u)):
                    free_bank(l, key)
                    if kind == "swa":
                        exp_done.wait(pe, l, (u, 2 * a + 1))
                        for kv in range(KV_SWA):
                            for kb in range(2 - swa_keys(i)[0], 2):
                                c = 256 * kv + P * kb
                                last = nc.tensor.transpose(bank(key)[:, c:c + P], PS[:, 512 * a + c:512 * a + c + P],
                                                           IDENT)
                    elif kind == "ca":
                        exp_done.wait(pe, l, (u, a))
                        for kb in range(i + 1):
                            last = nc.tensor.transpose(bank(key)[:, P * kb:P * kb + P],
                                                       PC[:, 512 * a + P * kb:512 * a + P * kb + P], IDENT)
                    elif kind == "swa sample":
                        probs_scaled.wait(pe, l, u)
                        for c in range(4):
                            j = 4 * a + c
                            src = PS_ROWS[:, j, 0:SWA_CACHE] if j < STREAMS else ZS[0:SWA_ROWS, j - STREAMS, :]
                            last = nc.tensor.transpose(bank(key)[:, SWA_ROWS * c:SWA_ROWS * (c + 1)], src,
                                                       IDENT[0:SWA_ROWS, 0:SWA_ROWS])
                    else:
                        probs_scaled.wait(pe, l, u)
                        p0 = (i % 2) * CA_WIDTH
                        for c in range(1 if a else 4):
                            src = ZC[:, i, :] if a else PC[:, p0 + P * c:p0 + P * (c + 1)]
                            last = nc.tensor.transpose(bank(key)[:, P * c:P * (c + 1)], src, IDENT)
                    att_done.done(last, key)

            def outs(l, u):
                kind, i = u
                for a, key in enumerate(out_jobs(u)):
                    free_bank(l, key)
                    turned_jobs = turn_jobs(u)
                    out_act.wait(pe, l, turned_jobs[-1])
                    if kind == "swa":
                        first = 2 - swa_keys(i)[0]
                        for g in range(G_SWA):
                            for kv in range(KV_SWA):
                                out = bank(key)[:, 64 * (2 * g + kv):64 * (2 * g + kv + 1)]
                                for kb in range(first, 2):
                                    c = 512 * g + 256 * kv + P * kb
                                    last = mm(out, PTS[:, c:c + P], T[:, i - 1 + kb, SWA_V, 64 * kv:64 * kv + 64],
                                              start=kb == first, stop=kb == 1)
                    elif kind == "ca":
                        for h in range(H_CA):
                            for kb in range(i + 1):
                                last = mm(bank(key)[:, 64 * h:64 * h + 64], PTC[:, 512 * h + P * kb:512 * h + P * kb + P],
                                          T[:, kb, CA_V + h // 2, 64 * (h % 2):64 * (h % 2) + 64],
                                          start=kb == 0, stop=kb == i)
                    elif kind == "swa sample":
                        for b in range(4 * a, 4 * a + 4):
                            out = bank(key)[:, SWA_ROWS * (b - 4 * a):SWA_ROWS * (b - 4 * a + 1)]
                            mm(out, SWV[:, b, :], PTS[:, SWA_ROWS * b:SWA_ROWS * (b + 1)], stop=False)
                            last = mm(out, T[:, SAMPLE, SWA_V, :],
                                      PTS[:, SWA_ROWS * (STREAMS + b):SWA_ROWS * (STREAMS + b + 1)], start=False)
                    else:
                        for b2 in range(2):
                            pe.wait_ge(cav_loaded[b2], 16 * (4 * l + i + 1))
                            for pair in range(2):
                                r0 = 32 * (2 * b2 + pair)
                                for tb in range(5):
                                    c = 640 * (i % 2) + P * tb + r0
                                    v = (CAV[:, b2, tb, P * pair:P * (pair + 1)] if tb < 4
                                         else T[:, SAMPLE, CA_V + pair, :])
                                    last = mm(bank(key, P)[r0:r0 + 32], PTC[:, c:c + 32], v, start=tb == 0, stop=tb == 4)
                    att_done.done(last, key)

            for s in unit_used:
                nc.tensor.sem_inc(s, CREDIT)
            pe.wait_ge(const_loaded, 16)
            with pe.Fori(0, DEPTH) as l:
                for u in range(IN_TILES):
                    if u >= 2:
                        in_copied.wait(pe, l, u - 2)
                    ready = (lambda k: normed_lo.wait(pe, l, ("mix", k))) if u == 0 else None
                    product(l, u, XNH, XNL, 2 * (u % 2), ready=ready)
                    if u == 0:
                        sum_columns(l, "mix")
                    if u - 1 in TOKEN_SLOT:
                        turn_tile(l, u - 1)
                turn_tile(l, IN_TILES - 1)
                in_copied.wait(pe, l, IN_TILES - 1)
                token_ready.wait(pe, l, TOKEN_TILES[-1])
                gates_ready.wait(pe, l, GATE_TILES[-1])
                rotary_step.wait(pe, l, (SAMPLE, 4))
                for s in range(6):
                    for b in range(PROMPT_BLOCKS):
                        last = nc.tensor.transpose(bank(("turn qk", s))[:, P * b:P * b + P], T[:, b, s, :], IDENT)
                    att_done.done(last, ("turn qk", s))
                for a in range(2):
                    for c in range(2 if a else 4):
                        last = nc.tensor.transpose(bank(("turn qk sample", a))[:, P * c:P * c + P],
                                                   T[:, SAMPLE, 4 * a + c, :], IDENT)
                    att_done.done(last, ("turn qk sample", a))
                out_act.wait(pe, l, ("turn qk", 4))
                out_dve.wait(pe, l, ("turn qk sample", 1))
                for b in range(BLOCKS):
                    if b == SAMPLE:
                        pe.wait_ge(states_loaded, 16 * (l + 1))
                    retention(l, b)
                pe.wait_ge(rel_loaded, 16 * (l + 1))
                for h in range(H_CA):
                    free_bank(l, ("bias", h))
                    att_done.done(mm(bank(("bias", h)), FLIP, PTC[:, 512 * h:512 * (h + 1)]), ("bias", h))
                pe.wait_ge(rel_rows_loaded, 16 * 8 * (l + 1))
                for a in range(2):
                    cols = slice(CA_CACHE, CA_WIDTH) if a else slice(0, CA_CACHE)
                    free_bank(l, ("bias rows", a))
                    att_done.done(mm(bank(("bias rows", a), STEP if a else CA_CACHE), FLIP16, PS[:, cols]),
                                  ("bias rows", a))
                for u in ATT_UNITS[:2]:
                    scores(l, u)
                for n, u in enumerate(ATT_UNITS):
                    turns(l, u)
                    for v in ATT_UNITS[n + 2:n + 3]:
                        scores(l, v)
                    outs(l, u)
                free_bank(l, ("cas back",))
                out_dve.wait(pe, l, ("cas out", 3))
                for i in range(4):
                    last = nc.tensor.transpose(bank(("cas back",))[:, P * i:P * (i + 1)], CO[:, i, :], IDENT)
                att_done.done(last, ("cas back",))
                ret_stat.wait(pe, l, "gated")
                for b, a in MIX_JOBS:
                    key = ("mix", b, a)
                    free_bank(l, key)
                    if b < SAMPLE and a == 0:
                        out_dve.wait(pe, l, max((("ca out", b), ("swa out", b)), key=order.get))
                    for c in range(4 if b < SAMPLE else 3):
                        t = 4 * a + c
                        slot = RET_OUT + t if t < 3 else t - 3
                        last = nc.tensor.transpose(bank(key)[:, P * c:P * c + P], T[:, b, slot, :], IDENT)
                    att_done.done(last, key)
                out_dve.wait(pe, l, ("mix", SAMPLE, 0))
                mixed_sample_lo.wait(pe, l, "sample")
                for m in range(KT):
                    if m >= 2:
                        pe.wait_ge(residual, l * RESIDUALS + KT + m - 1)
                    product(l, OUT_UNIT + m, XNH, XNL, 2 * (m % 2))
                def gate(h, f, ready=None):
                    pe.wait_ge(gate_copied, CREDIT + 2 * (l * FF_TILES + h * FF_HALF + f))
                    product(l, FFN_UNIT, XNH, XNL, 0, h * FFN_EXTRA + f, ready=ready)

                def up(h, f):
                    pe.wait_ge(up_copied, CREDIT + l * FF_TILES + h * FF_HALF + f)
                    product(l, FFN_UNIT + 1, XNH, XNL, 2, h * FFN_EXTRA + f)

                pe.wait_ge(residual, l * RESIDUALS + 2 * KT)
                gate(0, 0, ready=lambda k: normed_lo.wait(pe, l, ("ffn", k)))
                sum_columns(l, "ffn")
                up(0, 0)
                for h in range(FFN_HALVES):
                    with pe.Fori(0 if h else 1, FF_HALF) as f:
                        gate(h, f)
                        up(h, f)
                    with pe.Fori(0, KT // 2) as m2:
                        pe.wait_ge(y_lo, CREDIT + l * FF_TILES + h * FF_HALF + DOWN_SPLIT[0])
                        for j in range(2):
                            extra = h * FFN_EXTRA + 2 * m2 + j
                            b = 4 + 2 * j
                            pe.wait_ge(residual, l * RESIDUALS + KT + KT + KT * h + 2 * m2 + j - 1)
                            product(l, DOWN_UNIT, YH, YL, b, extra, tiles=DOWN_SPLIT[0], stop=False)
                            if j == 0:
                                pe.wait_ge(y_lo, CREDIT + l * FF_TILES + (h + 1) * FF_HALF)
                            product(l, DOWN_UNIT + 1, YH, YL, b, extra, tiles=DOWN_SPLIT[1], first=DOWN_SPLIT[0],
                                    start=False)
            squares_step.wait(pe, DEPTH, ("mix", 2 * KT - 2))
            for a in range(2):
                last = nc.tensor.matmul(PSUM[:, a, 0:HALF], ONES, ACC[:, HALF * a:HALF * (a + 1)], start=True, stop=True)
            last.then_inc(column_sums.sem, 1)


def _constants():
    import numpy as np

    f32 = np.float32
    c = np.zeros((P, N_CONST), f32)
    p = np.arange(P)

    def put(name, value):
        c[:, _C[name][0]:_C[name][1]] = np.asarray(value, f32).reshape(P, -1)

    put("ident", np.eye(P))
    put("ones", np.ones((P, P)))
    put("flip", np.eye(P)[::-1])
    flip16 = np.zeros((P, P))
    flip16[p, STEP * (p // STEP) + STEP - 1 - p % STEP] = 1.0
    put("flip16", flip16)
    half = HEAD_DIM // 2
    inv = f32(1.0) / (f32(10000.0) ** (np.arange(half, dtype=f32) / f32(half)))
    pos = np.concatenate([np.arange(SEQ), 1024 + np.tile(np.arange(STEP), STREAMS)]).astype(f32)
    angle = (pos[:, None] * inv[None, :]).astype(f32).astype(np.float64)
    cos, sin = np.cos(angle), np.sin(angle)
    put("cos", np.concatenate([cos, cos], 1).reshape(BLOCKS, P, HEAD_DIM).transpose(1, 0, 2))
    put("sin", np.concatenate([-sin, sin], 1).reshape(BLOCKS, P, HEAD_DIM).transpose(1, 0, 2))
    g = 1.0 - 2.0 ** (-5.0 - np.arange(H_RET))
    decay = np.zeros((P, 2, 2, H_RET))
    for a, t in enumerate((p, p % STEP)):
        decay[:, a, 0] = g[None, :] ** (t[:, None] + 1)
        decay[:, a, 1] = SCALE * g[None, :] ** -(t[:, None] + 1.0)
    put("decay", decay)
    causal = p[:, None] <= p[None, :]
    put("causal", causal)
    put("causal_sample", causal & (p[:, None] // STEP == p[None, :] // STEP))
    chunk = (p >= 64)[:, None]
    n = np.arange(2 * P)[None, :]
    put("window", np.where(np.where(chunk, n < 64, n >= 192), NEG_INF, 0.0))
    put("stream", p[:, None] // STEP == np.arange(STREAMS)[None, :])
    put("block_decay", np.stack([g[2 * s + (p >= 64)] ** P for s in range(3)], 1))
    put("eps", np.full((P, 1), EPS))
    return c


def kernel(x_prompt, x_sample, cache_swa_k, cache_swa_v, cache_ca_k, cache_ca_v, state_ret, state_ffn_conv, w_in,
           w_out, attn_sinks, rel_bias_table, norm_mix, norm_ffn, w_gate, w_up, conv_w, conv_b, w_down, norm_final):
    import numpy as np
    import concourse.bacc as bacc
    from concourse.bass_utils import run_bass_kernel_spmd

    L, S = DEPTH, STREAMS
    a = {k: np.asarray(v) for k, v in locals().items() if k not in ("np", "bacc", "run_bass_kernel_spmd", "L", "S")}
    xp, xs = a["x_prompt"].reshape(2, HALF_PROMPT, D_MODEL), a["x_sample"].reshape(2, HALF_SAMPLE, D_MODEL)
    x = np.concatenate([xp, xs], axis=1).reshape(FRAMES, KT, P).transpose(2, 1, 0)

    def tiles(w, n):
        return w.reshape(L, w.shape[1] // P, P, n, P).transpose(0, 3, 2, 1, 4)

    q0 = 4 * H_RET * HEAD_DIM
    q1 = q0 + H_SWA * HEAD_DIM

    def pair_heads(w, axis):
        shape = w.shape
        w = w.reshape(*shape[:axis], KV_SWA, G_SWA, HEAD_DIM, *shape[axis + 1:])
        return np.swapaxes(w, axis, axis + 1).reshape(shape)

    wi = np.concatenate([a["w_in"][:, :, :q0], pair_heads(a["w_in"][:, :, q0:q1], 2), a["w_in"][:, :, q1:]], axis=2)
    o0 = H_RET * HEAD_DIM
    o1 = o0 + H_SWA * HEAD_DIM
    wo = np.concatenate([a["w_out"][:, :o0], pair_heads(a["w_out"][:, o0:o1], 1), a["w_out"][:, o1:]], axis=1)
    w_gu = np.stack([tiles(a["w_gate"], FF_TILES), tiles(a["w_up"], FF_TILES)], axis=2)
    w_gu = w_gu.reshape(L, FFN_HALVES, FF_HALF, 2, P, KT * P)
    wd = a["w_down"].reshape(L, FFN_HALVES, FF_HALF, P, KT, P).transpose(0, 1, 4, 3, 2, 5)
    w_dn = np.zeros((L, FFN_HALVES, KT, 2, P, DOWN_SPLIT[0], P), wd.dtype)
    w_dn[:, :, :, 0] = wd[..., :DOWN_SPLIT[0], :]
    w_dn[:, :, :, 1, :, :DOWN_SPLIT[1]] = wd[..., DOWN_SPLIT[0]:, :]
    sinks = a["attn_sinks"].reshape(L, KV_SWA, G_SWA).transpose(0, 2, 1).reshape(L, H_SWA)
    reversed_bias = a["rel_bias_table"].transpose(0, 2, 1)[:, :, ::-1]
    ck = a["cache_ca_k"].reshape(L, S, CA_CACHE, 2, P).transpose(0, 1, 4, 3, 2)
    cv = a["cache_ca_v"].reshape(L, S, 4, P, 2 * P).transpose(0, 1, 3, 2, 4)
    ins = {
        "x_in": x, "consts": _constants(),
        "w_in": tiles(wi, IN_TILES).reshape(L, IN_TILES, P, KT * P), "w_out": tiles(wo, KT).reshape(L, KT, P, KT * P),
        "w_gu": w_gu, "w_down": w_dn.reshape(L, FFN_HALVES, KT, 2, P, DOWN_SPLIT[0] * P),
        "gains": np.stack([a["norm_mix"], a["norm_ffn"]], 1).reshape(L, 2, KT, P).transpose(3, 0, 1, 2),
        "gain_final": a["norm_final"].reshape(KT, P).T,
        "conv_par": np.concatenate([a["conv_w"], a["conv_b"][:, None]], 1).reshape(L, 4, FF_TILES, P)
        .transpose(3, 0, 2, 1),
        "sinks": sinks, "sinks_rows": a["attn_sinks"],
        "rel": np.pad(reversed_bias, ((0, 0), (0, 0), (REL_PAD, 0)), mode="edge"),
        "swa_kt": a["cache_swa_k"].reshape(L, S, SWA_CACHE, P).transpose(0, 3, 1, 2),
        "swa_v": a["cache_swa_v"].reshape(L, S, SWA_CACHE, P).transpose(0, 2, 1, 3),
        "ca_kt": ck, "ca_v": cv,
        "ret_state": a["state_ret"].reshape(L, 4, 2, H_RET, HEAD_DIM, HEAD_DIM).transpose(0, 2, 4, 1, 3, 5)
        .reshape(L, P, 4, H_RET, HEAD_DIM),
        "conv_state": a["state_ffn_conv"].reshape(L, S, 2, FF_TILES, P).transpose(0, 4, 3, 1, 2),
    }
    outs = {
        "y_out": (P, KT, FRAMES), "feat_out": (L, P, 8, FRAMES), "tokv_out": (L, P, BLOCKS, 3, P),
        "ret_p_out": (L, P, 3, HEAD_DIM), "ret_s_out": (L, P, 4, H_RET, HEAD_DIM),
        "conv_out": (L, P, FF_TILES, 2 + 2 * S),
        "swa_kt_copy": (L, P, S, SWA_CACHE), "swa_v_copy": (L, P, S, P),
        "ca_kt_copy": ck.shape, "ca_v_copy": cv.shape,
    }
    nc = bacc.Bacc("TRN2", target_bir_lowering=False, num_devices=1)
    args, arrays = [], {}
    for name, value in ins.items():
        value = np.ascontiguousarray(value)
        arrays[name] = value
        args.append(nc.dram_tensor(name, value.shape, mybir.dt.from_np(value.dtype), kind="ExternalInput").ap())
    for name, shape in outs.items():
        args.append(nc.dram_tensor(name, shape, F32, kind="ExternalOutput").ap())
    build(nc, *args)
    r = run_bass_kernel_spmd(nc, [arrays], core_ids=[0]).results[0]

    y = np.asarray(r["y_out"]).transpose(2, 1, 0).reshape(2, HALF, D_MODEL)
    y_prompt = y[:, :HALF_PROMPT].reshape(1, SEQ, D_MODEL)
    y_sample = y[:, HALF_PROMPT:].reshape(S, STEP, D_MODEL)
    feat, tokv = np.asarray(r["feat_out"]), np.asarray(r["tokv_out"])
    k_swa = feat[:, :, SWA_K].transpose(0, 2, 1).reshape(L, FRAMES, KV_SWA, HEAD_DIM)
    k_ca = feat[:, :, CA_K:CA_K + 2].transpose(0, 3, 2, 1).reshape(L, FRAMES, H_CA, HEAD_DIM)
    v = tokv.transpose(0, 2, 1, 3, 4).reshape(L, FRAMES, 3 * P)
    v_swa = v[:, :, :P].reshape(L, FRAMES, KV_SWA, HEAD_DIM)
    v_ca = v[:, :, P:].reshape(L, FRAMES, H_CA, HEAD_DIM)

    def prompt(rows, n):
        return rows[:, None, SEQ - n:SEQ]

    def sample(cache, rows):
        return np.concatenate([cache[:, :, STEP:], rows[:, SEQ:].reshape(L, S, STEP, *rows.shape[2:])], axis=2)

    old_k = np.asarray(r["swa_kt_copy"]).transpose(0, 2, 3, 1).reshape(L, S, SWA_CACHE, KV_SWA, HEAD_DIM)
    old_v = np.asarray(r["swa_v_copy"]).transpose(0, 2, 1, 3).reshape(L, S, SWA_CACHE, KV_SWA, HEAD_DIM)
    old_ck = np.asarray(r["ca_kt_copy"]).transpose(0, 1, 4, 3, 2).reshape(L, S, CA_CACHE, H_CA, HEAD_DIM)
    old_cv = np.asarray(r["ca_v_copy"]).transpose(0, 1, 3, 2, 4).reshape(L, S, CA_CACHE, H_CA, HEAD_DIM)
    ret_p = np.asarray(r["ret_p_out"]).reshape(L, 2, HEAD_DIM, 3, HEAD_DIM).transpose(0, 3, 1, 2, 4)
    ret_s = np.asarray(r["ret_s_out"]).reshape(L, 2, HEAD_DIM, 4, H_RET, HEAD_DIM).transpose(0, 3, 1, 4, 2, 5)
    tails = np.asarray(r["conv_out"]).transpose(0, 3, 2, 1).reshape(L, 2 + 2 * S, D_FF)
    return (y_prompt, y_sample, prompt(k_swa, SWA_CACHE), prompt(v_swa, SWA_CACHE), prompt(k_ca, CA_CACHE),
            prompt(v_ca, CA_CACHE), ret_p.reshape(L, 1, H_RET, HEAD_DIM, HEAD_DIM), tails[:, None, :2],
            sample(old_k, k_swa), sample(old_v, v_swa), sample(old_ck, k_ca), sample(old_cv, v_ca),
            ret_s.reshape(L, S, H_RET, HEAD_DIM, HEAD_DIM), tails[:, 2:].reshape(L, S, 2, D_FF))
```
